# Optimizing a Trainium2 kernel written in Bass

```python
import math
import jax, jax.numpy as jnp
from jax import lax
import numpy as np

D_MODEL = 1024
BATCH = 1
SEQ = 512
DEPTH = 1

CHUNK = 64
Q_BLOCK = 128
N_MEM = 256
HEAD_DIM = 64
A_HEADS = 4
A_QK_DIM = HEAD_DIM
A_V_DIM = 2 * HEAD_DIM
B_HEADS = 8
B_DIM = HEAD_DIM
B_LEFT_CHUNKS = 8
B_BAND = B_LEFT_CHUNKS + 1
REL_CLIP = 128
C_HEADS = 4
C_DIM = 128
D_FF = 2816
ROPE_THETA = 10000.0
EPS = 1e-6
NEG = -1e30
N_BRANCH = 3

A_Q = A_HEADS * 2 * A_QK_DIM
A_V = A_HEADS * A_V_DIM
B_W = B_HEADS * B_DIM
C_W = C_HEADS * C_DIM
BRANCH_W = 512
IN_COLS = 2 * A_Q + A_V + 3 * B_W + C_W


def rmsnorm(x, g):
    xf = x.astype(jnp.float32)
    y = xf * lax.rsqrt(jnp.mean(xf * xf, axis=-1, keepdims=True) + EPS)
    return (y * g.astype(jnp.float32)).astype(x.dtype)

def rope(x):
    s, d = x.shape[1], x.shape[-1]
    half = d // 2
    inv = ROPE_THETA ** (-jnp.arange(half, dtype=jnp.float32) / half)
    ang = jnp.arange(s, dtype=jnp.float32)[:, None] * inv[None, :]
    shp = (1, s) + (1,) * (x.ndim - 3) + (half,)
    cos, sin = jnp.cos(ang).reshape(shp), jnp.sin(ang).reshape(shp)
    xf = x.astype(jnp.float32)
    x1, x2 = xf[..., :half], xf[..., half:]
    return jnp.concatenate([x1 * cos - x2 * sin, x2 * cos + x1 * sin], axis=-1).astype(x.dtype)

def swiglu(h, wg, wu, wd):
    return (jax.nn.silu(h @ wg) * (h @ wu)) @ wd

def diff_attention(q, k, v, lam, lambda_init, sub_gain):
    b, s, h = q.shape[0], q.shape[1], q.shape[2]
    scale = A_QK_DIM ** -0.5
    chunk_id = jnp.arange(s) // CHUNK
    outs = []
    for i in range(s // Q_BLOCK):
        q0, q1 = i * Q_BLOCK, (i + 1) * Q_BLOCK
        kb, vb = k[:, :q1], v[:, :q1]
        sc = jnp.einsum('bqhcd,bkhcd->bhcqk', q[:, q0:q1], kb).astype(jnp.float32) * scale
        mask = chunk_id[q0:q1, None] >= chunk_id[None, :q1]
        sc = jnp.where(mask[None, None, None], sc, NEG)
        p = jax.nn.softmax(sc, axis=-1)
        a = p[:, :, 0] - lam * p[:, :, 1]
        outs.append(jnp.einsum('bhqk,bkhd->bqhd', a.astype(v.dtype), vb))
    o = jnp.concatenate(outs, axis=1)
    o = rmsnorm(o, sub_gain) * (1.0 - lambda_init)
    return o.reshape(b, s, h * A_V_DIM)

def chunk_band_attention(q, k, v, rel_table):
    b, s, h, d = q.shape
    nc = s // CHUNK
    scale = d ** -0.5
    qc = q.reshape(b, nc, CHUNK, h, d)
    pad = ((0, 0), (B_LEFT_CHUNKS, 0), (0, 0), (0, 0), (0, 0))
    kp = jnp.pad(k.reshape(b, nc, CHUNK, h, d), pad)
    vp = jnp.pad(v.reshape(b, nc, CHUNK, h, d), pad)
    band_idx = jnp.arange(nc)[:, None] + jnp.arange(B_BAND)[None, :]
    kb = kp[:, band_idx].reshape(b, nc, B_BAND * CHUNK, h, d)
    vb = vp[:, band_idx].reshape(b, nc, B_BAND * CHUNK, h, d)
    sc = jnp.einsum('bcqhd,bckhd->bchqk', qc, kb).astype(jnp.float32) * scale
    qpos = jnp.arange(CHUNK) + B_LEFT_CHUNKS * CHUNK
    kpos = jnp.arange(B_BAND * CHUNK)
    rel = jnp.clip(qpos[:, None] - kpos[None, :], -REL_CLIP, REL_CLIP) + REL_CLIP
    sc = sc + rel_table.astype(jnp.float32)[:, rel][None, None]
    valid = jnp.repeat(band_idx >= B_LEFT_CHUNKS, CHUNK, axis=1)
    sc = jnp.where(valid[None, :, None, None, :], sc, NEG)
    p = jax.nn.softmax(sc, axis=-1)
    o = jnp.einsum('bchqk,bckhd->bcqhd', p.astype(v.dtype), vb)
    return o.reshape(b, s, h * d)

def memory_attention(q, mk, mv):
    b, s, h, d = q.shape
    sc = jnp.einsum('bshd,bmhd->bhsm', q, mk).astype(jnp.float32) * (d ** -0.5)
    p = jax.nn.softmax(sc, axis=-1)
    return jnp.einsum('bhsm,bmhd->bshd', p.astype(mv.dtype), mv).reshape(b, s, h * d)

def first_inputs(seed: int = 0) -> dict:
    key = jax.random.key(seed)
    ks = iter(jax.random.split(key, 40))
    L, D, F = DEPTH, D_MODEL, D_FF

    def w(shape, fan_in):
        return jax.random.normal(next(ks), shape, jnp.float32) * (fan_in ** -0.5)

    def gain(shape):
        return 1.0 + 0.01 * jax.random.normal(next(ks), shape, jnp.float32)

    def small(shape, s):
        return s * jax.random.normal(next(ks), shape, jnp.float32)

    return {
        "x": jax.random.normal(next(ks), (BATCH, SEQ, D), jnp.float32),
        "mem": jax.random.normal(next(ks), (BATCH, N_MEM, D), jnp.float32),
        "ffn1_norm": gain((L, D)),
        "ffn1_wg": w((L, D, F), D),
        "ffn1_wu": w((L, D, F), D),
        "ffn1_wd": w((L, F, D), F),
        "mix_norm": gain((L, D)),
        "w_in": w((L, D, IN_COLS), D),
        "a_q_norm": gain((L, A_QK_DIM)),
        "a_k_norm": gain((L, A_QK_DIM)),
        "a_lambda": small((L, 4, A_QK_DIM), 0.1),
        "a_sub_norm": gain((L, A_V_DIM)),
        "b_q_norm": gain((L, B_DIM)),
        "b_k_norm": gain((L, B_DIM)),
        "b_rel_bias": small((L, B_HEADS, 2 * REL_CLIP + 1), 0.1),
        "mem_norm": gain((L, D)),
        "w_mem_kv": w((L, D, 2 * C_W), D),
        "c_q_norm": gain((L, C_DIM)),
        "c_k_norm": gain((L, C_DIM)),
        "w_gate": w((L, D, N_BRANCH * D), D),
        "b_gate": small((L, N_BRANCH * D), 0.01),
        "w_branch": w((L, N_BRANCH, BRANCH_W, D), BRANCH_W),
        "w_out": w((L, D, D), D),
        "ffn2_norm": gain((L, D)),
        "ffn2_wg": w((L, D, F), D),
        "ffn2_wu": w((L, D, F), D),
        "ffn2_wd": w((L, F, D), F),
        "final_norm": gain((L, D)),
    }

def first_block(x, mem, ffn1_norm, ffn1_wg, ffn1_wu, ffn1_wd, mix_norm, w_in,
              a_q_norm, a_k_norm, a_lambda, a_sub_norm, b_q_norm, b_k_norm, b_rel_bias,
              mem_norm, w_mem_kv, c_q_norm, c_k_norm, w_gate, b_gate, w_branch, w_out,
              ffn2_norm, ffn2_wg, ffn2_wu, ffn2_wd, final_norm):
    b, s, d = x.shape
    m = mem.shape[1]
    split_at = list(np.cumsum([A_Q, A_Q, A_V, B_W, B_W, B_W])) 
    for l in range(DEPTH):
        x = x + 0.5 * swiglu(rmsnorm(x, ffn1_norm[l]), ffn1_wg[l], ffn1_wu[l], ffn1_wd[l])

        h = rmsnorm(x, mix_norm[l])
        proj = h @ w_in[l]
        aq, ak, av, bq, bk, bv, cq = jnp.split(proj, [int(i) for i in split_at], axis=-1)

        lambda_init = 0.8 - 0.6 * math.exp(-0.3 * l)
        lp = a_lambda[l].astype(jnp.float32)
        lam = jnp.exp(jnp.sum(lp[0] * lp[1])) - jnp.exp(jnp.sum(lp[2] * lp[3])) + lambda_init
        aq = rope(rmsnorm(aq.reshape(b, s, A_HEADS, 2, A_QK_DIM), a_q_norm[l]))
        ak = rope(rmsnorm(ak.reshape(b, s, A_HEADS, 2, A_QK_DIM), a_k_norm[l]))
        av = av.reshape(b, s, A_HEADS, A_V_DIM)
        o_a = diff_attention(aq, ak, av, lam, lambda_init, a_sub_norm[l])

        bq = rmsnorm(bq.reshape(b, s, B_HEADS, B_DIM), b_q_norm[l])
        bk = rmsnorm(bk.reshape(b, s, B_HEADS, B_DIM), b_k_norm[l])
        bv = bv.reshape(b, s, B_HEADS, B_DIM)
        o_b = chunk_band_attention(bq, bk, bv, b_rel_bias[l])

        mkv = rmsnorm(mem, mem_norm[l]) @ w_mem_kv[l]
        mk, mv = jnp.split(mkv, 2, axis=-1)
        mk = rmsnorm(mk.reshape(b, m, C_HEADS, C_DIM), c_k_norm[l])
        mv = mv.reshape(b, m, C_HEADS, C_DIM)
        cq = rmsnorm(cq.reshape(b, s, C_HEADS, C_DIM), c_q_norm[l])
        o_c = memory_attention(cq, mk, mv)

        gates = jax.nn.sigmoid(h @ w_gate[l] + b_gate[l]).reshape(b, s, N_BRANCH, d)
        branches = jnp.stack([o_a, o_b, o_c], axis=2)
        y = jnp.einsum('bsnc,ncd,bsnd->bsd', branches, w_branch[l], gates)
        x = x + y @ w_out[l]

        x = x + 0.5 * swiglu(rmsnorm(x, ffn2_norm[l]), ffn2_wg[l], ffn2_wu[l], ffn2_wd[l])
        x = rmsnorm(x, final_norm[l])
    return x


_first_inputs = first_inputs


def first_inputs(seed=0):
    import zlib

    import numpy as np

    out = dict(_first_inputs(seed))
    spreads = {}
    factors = {'ffn1_norm': 8.0,
     'mix_norm': 7.6,
     'a_q_norm': 24.21,
     'a_k_norm': 22.442,
     'a_sub_norm': 64.0,
     'b_q_norm': 28.943,
     'b_k_norm': 25.71,
     'b_rel_bias': 21.395,
     'mem_norm': 22.082,
     'c_q_norm': 21.495,
     'c_k_norm': 22.217,
     'b_gate': 64.0,
     'ffn2_norm': 47.74,
     'final_norm': 38.903}
    for name, (base, spread) in spreads.items():
        noise = np.random.default_rng([zlib.crc32(name.encode()), seed]).standard_normal(out[name].shape)
        drawn = base * np.exp(spread * noise) if base else spread * noise
        out[name] = __import__('jax').numpy.asarray(drawn.astype(out[name].dtype))
    for name, factor in factors.items():
        out[name] = (out[name] * factor).astype(out[name].dtype)
    return out


_narrow_inputs = first_inputs


def first_inputs(seed=0):

    out = dict(_narrow_inputs(seed))
    wider = {'a_sub_norm': 5.32,
     'b_q_norm': 3.31,
     'b_k_norm': 3.05,
     'b_rel_bias': 7.81,
     'ffn2_norm': 4.6,
     'final_norm': 7.0}
    for name, times in wider.items():
        mean = out[name].mean()
        out[name] = (mean + times * (out[name] - mean)).astype(out[name].dtype)
    return out


MEM_LEN = 256
NSA_HEADS = 16
NSA_KV_GROUPS = 4
NSA_HPG = NSA_HEADS // NSA_KV_GROUPS
CMP_LEN = 32
CMP_STRIDE = 16
CMP_HIDDEN = 256
SEL_BLOCK = 64
SEL_TOPK = 8
WINDOW = 512
ROPE_THETA_2 = 500000.0
ROPE_DIM = HEAD_DIM // 4
RNN_WIDTH = D_MODEL
RNN_BLOCKS = 16
RNN_BLOCK_DIM = RNN_WIDTH // RNN_BLOCKS
CONV_WIDTH = 4
RGLRU_C = 8.0
XATTN_HEADS = 4
XATTN_WIDTH = XATTN_HEADS * HEAD_DIM
D_FF_2 = 4 * D_MODEL
N_BRANCHES = 3
RMS_EPS = 1e-6

NSA_Q = NSA_HEADS * HEAD_DIM
NSA_KV = NSA_KV_GROUPS * HEAD_DIM
NSA_GATES = NSA_HEADS * 3
IN_WIDTHS = (NSA_Q, NSA_KV, NSA_KV, NSA_KV, NSA_KV, NSA_KV, NSA_KV, NSA_GATES,
             RNN_WIDTH, RNN_WIDTH, XATTN_WIDTH, N_BRANCHES * D_MODEL)
D_IN = sum(IN_WIDTHS)


def rms_norm(x, g):
    xf = x.astype(jnp.float32)
    y = xf * lax.rsqrt(jnp.mean(xf * xf, axis=-1, keepdims=True) + RMS_EPS)
    return (y * g.astype(jnp.float32)).astype(x.dtype)

def masked_softmax(s, mask):
    s = jnp.where(mask, s.astype(jnp.float32), -jnp.inf)
    m = jnp.max(s, axis=-1, keepdims=True)
    m = jnp.where(jnp.isfinite(m), m, 0.0)
    e = jnp.exp(s - m)
    return e / jnp.maximum(jnp.sum(e, axis=-1, keepdims=True), 1e-30)

def rope_tables(pos):
    inv = 1.0 / (ROPE_THETA_2 ** (jnp.arange(0, ROPE_DIM, 2, dtype=jnp.float32) / ROPE_DIM))
    ang = pos.astype(jnp.float32)[:, None] * inv[None, :]
    return jnp.cos(ang), jnp.sin(ang)

def apply_partial_rope(x, cos, sin):
    half = ROPE_DIM // 2
    xf = x.astype(jnp.float32)
    x1 = xf[..., :half]
    x2 = xf[..., half:ROPE_DIM]
    out = jnp.concatenate([x1 * cos - x2 * sin, x2 * cos + x1 * sin, xf[..., ROPE_DIM:]], axis=-1)
    return out.astype(x.dtype)

def cmp_to_sel_weights(n_cmp, n_sel):
    c0 = np.arange(n_cmp)[:, None] * CMP_STRIDE
    s0 = np.arange(n_sel)[None, :] * SEL_BLOCK
    ov = np.clip(np.minimum(c0 + CMP_LEN, s0 + SEL_BLOCK) - np.maximum(c0, s0), 0, None)
    return (ov / CMP_LEN).astype(np.float32)

def compress_blocks(kv, pos_emb, w1, w2):
    B, G, S, hd = kv.shape
    n_cmp = (S - CMP_LEN) // CMP_STRIDE + 1
    idx = jnp.arange(n_cmp)[:, None] * CMP_STRIDE + jnp.arange(CMP_LEN)[None, :]
    blocks = kv[:, :, idx, :] + pos_emb
    flat = blocks.reshape(B, G, n_cmp, CMP_LEN * hd)
    return jax.nn.gelu(flat @ w1) @ w2

def nsa_mixer(q, k_c, v_c, k_s, v_s, k_w, v_w, gates):
    B, G, Hg, S, hd = q.shape
    n_cmp = k_c.shape[2]
    n_sel = S // SEL_BLOCK
    n_top = min(SEL_TOPK, n_sel)
    nq = S // Q_BLOCK
    scale = HEAD_DIM ** -0.5
    c2s = jnp.asarray(cmp_to_sel_weights(n_cmp, n_sel))
    cmp_end = jnp.arange(n_cmp) * CMP_STRIDE + (CMP_LEN - 1)
    ks_blocks = k_s.reshape(B, G, n_sel, SEL_BLOCK, hd)
    vs_blocks = v_s.reshape(B, G, n_sel, SEL_BLOCK, hd)
    kw_pad = jnp.pad(k_w, ((0, 0), (0, 0), (WINDOW, 0), (0, 0)))
    vw_pad = jnp.pad(v_w, ((0, 0), (0, 0), (WINDOW, 0), (0, 0)))
    bi = jnp.arange(B)[:, None, None, None]
    gi = jnp.arange(G)[None, :, None, None]
    blk_ids = jnp.arange(n_sel)

    def block(args):
        i, q_b, g_b = args
        t = i * Q_BLOCK + jnp.arange(Q_BLOCK)
        s_c = jnp.einsum('bghqd,bgnd->bghqn', q_b, k_c) * scale
        p_c = masked_softmax(s_c, cmp_end[None, :] <= t[:, None])
        o_c = jnp.einsum('bghqn,bgnd->bghqd', p_c.astype(q_b.dtype), v_c)
        imp = jnp.einsum('bghqn,ns->bgqs', p_c, c2s)
        cur = (t // SEL_BLOCK)[:, None]
        forced = (blk_ids == 0) | (blk_ids == cur) | (blk_ids == cur - 1)
        future = blk_ids * SEL_BLOCK > t[:, None]
        imp = jnp.where(forced, jnp.inf, jnp.where(future, -jnp.inf, imp))
        _, idx = lax.top_k(imp, n_top)
        k_g = ks_blocks[bi, gi, idx]
        v_g = vs_blocks[bi, gi, idx]
        key_pos = (idx[..., None] * SEL_BLOCK + jnp.arange(SEL_BLOCK)).reshape(B, G, 1, Q_BLOCK, n_top * SEL_BLOCK)
        s_s = jnp.einsum('bghqd,bgqkld->bghqkl', q_b, k_g).reshape(B, G, Hg, Q_BLOCK, n_top * SEL_BLOCK) * scale
        p_s = masked_softmax(s_s, key_pos <= t[:, None])
        o_s = jnp.einsum('bghqkl,bgqkld->bghqd',
                         p_s.astype(q_b.dtype).reshape(B, G, Hg, Q_BLOCK, n_top, SEL_BLOCK), v_g)
        start = i * Q_BLOCK
        k_b = lax.dynamic_slice_in_dim(kw_pad, start, Q_BLOCK + WINDOW, axis=2)
        v_b = lax.dynamic_slice_in_dim(vw_pad, start, Q_BLOCK + WINDOW, axis=2)
        w_pos = start - WINDOW + jnp.arange(Q_BLOCK + WINDOW)
        mask_w = (w_pos[None, :] <= t[:, None]) & (w_pos[None, :] > t[:, None] - WINDOW)
        s_w = jnp.einsum('bghqd,bgkd->bghqk', q_b, k_b) * scale
        p_w = masked_softmax(s_w, mask_w)
        o_w = jnp.einsum('bghqk,bgkd->bghqd', p_w.astype(q_b.dtype), v_b)
        return g_b[..., 0:1] * o_c + g_b[..., 1:2] * o_s + g_b[..., 2:3] * o_w

    q_blocks = jnp.moveaxis(q.reshape(B, G, Hg, nq, Q_BLOCK, hd), 3, 0)
    g_blocks = jnp.moveaxis(gates.reshape(B, G, Hg, nq, Q_BLOCK, 3), 3, 0)
    out = lax.map(block, (jnp.arange(nq), q_blocks, g_blocks))
    out = jnp.moveaxis(out, 0, 3).reshape(B, G, Hg, S, hd)
    return out.transpose(0, 3, 1, 2, 4).reshape(B, S, G * Hg * hd)

def causal_depthwise_conv(x, w, b):
    S = x.shape[1]
    xp = jnp.pad(x, ((0, 0), (CONV_WIDTH - 1, 0), (0, 0)))
    y = b
    for k in range(CONV_WIDTH):
        y = y + xp[:, k:k + S, :] * w[k]
    return y

def rg_lru(xr, w_a, b_a, w_i, b_i, lam):
    B, S, C = xr.shape
    xb = xr.reshape(B, S, RNN_BLOCKS, RNN_BLOCK_DIM)
    r = jax.nn.sigmoid(jnp.einsum('bsnk,nkj->bsnj', xb, w_a).reshape(B, S, C) + b_a)
    gi = jax.nn.sigmoid(jnp.einsum('bsnk,nkj->bsnj', xb, w_i).reshape(B, S, C) + b_i)
    log_a = -RGLRU_C * r.astype(jnp.float32) * jax.nn.softplus(-lam.astype(jnp.float32))
    a = jnp.exp(log_a)
    mult = jnp.sqrt(-jnp.expm1(2.0 * log_a))
    u = mult * (gi * xr).astype(jnp.float32)

    def combine(c1, c2):
        a1, b1 = c1
        a2, b2 = c2
        return a1 * a2, a2 * b1 + b2

    _, h = lax.associative_scan(combine, (a, u), axis=1)
    return h.astype(xr.dtype)

def cross_attention(q_x, mem, g_mem, w_mem_kv, w_xo):
    B, S, _ = q_x.shape
    M = mem.shape[1]
    q = q_x.reshape(B, S, XATTN_HEADS, HEAD_DIM)
    kv = (rms_norm(mem, g_mem) @ w_mem_kv).reshape(B, M, 2, XATTN_HEADS, HEAD_DIM)
    s = jnp.einsum('bshd,bmhd->bhsm', q, kv[:, :, 0]) * (HEAD_DIM ** -0.5)
    p = jax.nn.softmax(s.astype(jnp.float32), axis=-1).astype(q.dtype)
    o = jnp.einsum('bhsm,bmhd->bshd', p, kv[:, :, 1]).reshape(B, S, XATTN_WIDTH)
    return o @ w_xo

def second_inputs(seed: int = 0) -> dict:
    key = jax.random.key(seed)
    ks = jax.random.split(key, 32)
    L = DEPTH

    def nrm(k, shape, fan_in):
        return jax.random.normal(k, shape, jnp.float32) * (fan_in ** -0.5)

    def gain(k, shape):
        return 1.0 + 0.02 * jax.random.normal(k, shape, jnp.float32)

    def small(k, shape):
        return 0.02 * jax.random.normal(k, shape, jnp.float32)

    u = jax.random.uniform(ks[20], (L, RNN_WIDTH), jnp.float32, 0.9, 0.999) ** (1.0 / RGLRU_C)
    rg_lambda = jnp.log(u) - jnp.log1p(-u)
    return {
        "x": jax.random.normal(ks[0], (BATCH, SEQ, D_MODEL), jnp.float32),
        "mem": jax.random.normal(ks[1], (BATCH, MEM_LEN, D_MODEL), jnp.float32),
        "g_mix": gain(ks[2], (L, D_MODEL)),
        "w_in": nrm(ks[3], (L, D_MODEL, D_IN), D_MODEL),
        "cmp_pos_k": small(ks[4], (L, CMP_LEN, HEAD_DIM)),
        "cmp_pos_v": small(ks[5], (L, CMP_LEN, HEAD_DIM)),
        "w_cmp_k1": nrm(ks[6], (L, CMP_LEN * HEAD_DIM, CMP_HIDDEN), CMP_LEN * HEAD_DIM),
        "w_cmp_k2": nrm(ks[7], (L, CMP_HIDDEN, HEAD_DIM), CMP_HIDDEN),
        "w_cmp_v1": nrm(ks[8], (L, CMP_LEN * HEAD_DIM, CMP_HIDDEN), CMP_LEN * HEAD_DIM),
        "w_cmp_v2": nrm(ks[9], (L, CMP_HIDDEN, HEAD_DIM), CMP_HIDDEN),
        "conv_w": nrm(ks[10], (L, CONV_WIDTH, RNN_WIDTH), CONV_WIDTH),
        "conv_b": small(ks[11], (L, RNN_WIDTH)),
        "w_rg_a": nrm(ks[12], (L, RNN_BLOCKS, RNN_BLOCK_DIM, RNN_BLOCK_DIM), RNN_BLOCK_DIM),
        "b_rg_a": small(ks[13], (L, RNN_WIDTH)),
        "w_rg_i": nrm(ks[14], (L, RNN_BLOCKS, RNN_BLOCK_DIM, RNN_BLOCK_DIM), RNN_BLOCK_DIM),
        "b_rg_i": small(ks[15], (L, RNN_WIDTH)),
        "rg_lambda": rg_lambda,
        "g_mem": gain(ks[16], (L, D_MODEL)),
        "w_mem_kv": nrm(ks[17], (L, D_MODEL, 2 * XATTN_WIDTH), D_MODEL),
        "w_xo": nrm(ks[18], (L, XATTN_WIDTH, D_MODEL), XATTN_WIDTH),
        "w_o": nrm(ks[19], (L, D_MODEL, D_MODEL), D_MODEL),
        "g_mlp": gain(ks[21], (L, D_MODEL)),
        "w_up": nrm(ks[22], (L, D_MODEL, D_FF_2), D_MODEL),
        "w_down": nrm(ks[23], (L, D_FF_2, D_MODEL), D_FF_2),
        "g_final": gain(ks[24], (D_MODEL,)),
    }

def second_block(x, mem, g_mix, w_in, cmp_pos_k, cmp_pos_v, w_cmp_k1, w_cmp_k2, w_cmp_v1, w_cmp_v2,
              conv_w, conv_b, w_rg_a, b_rg_a, w_rg_i, b_rg_i, rg_lambda, g_mem, w_mem_kv, w_xo,
              w_o, g_mlp, w_up, w_down, g_final):
    B, S, D = x.shape
    G, Hg, hd = NSA_KV_GROUPS, NSA_HPG, HEAD_DIM
    offsets = np.cumsum(IN_WIDTHS)[:-1].tolist()
    cos, sin = rope_tables(jnp.arange(S))
    n_cmp = (S - CMP_LEN) // CMP_STRIDE + 1
    cos_c, sin_c = rope_tables(jnp.arange(n_cmp) * CMP_STRIDE + (CMP_LEN - 1))

    def to_groups(t):
        return t.reshape(B, S, G, hd).transpose(0, 2, 1, 3)

    h = x
    for l in range(DEPTH):
        u = rms_norm(h, g_mix[l])
        z = u @ w_in[l]
        (q_n, kc_raw, vc_raw, k_s, v_s, k_w, v_w, nsa_g,
         x_rnn, g_rnn, q_x, merge_g) = jnp.split(z, offsets, axis=-1)

        q = q_n.reshape(B, S, G, Hg, hd).transpose(0, 2, 3, 1, 4)
        q = apply_partial_rope(q, cos, sin)
        k_s = apply_partial_rope(to_groups(k_s), cos, sin)
        k_w = apply_partial_rope(to_groups(k_w), cos, sin)
        k_c = compress_blocks(to_groups(kc_raw), cmp_pos_k[l], w_cmp_k1[l], w_cmp_k2[l])
        k_c = apply_partial_rope(k_c, cos_c, sin_c)
        v_c = compress_blocks(to_groups(vc_raw), cmp_pos_v[l], w_cmp_v1[l], w_cmp_v2[l])
        nsa_gates = jax.nn.sigmoid(nsa_g).reshape(B, S, G, Hg, 3).transpose(0, 2, 3, 1, 4)
        y_nsa = nsa_mixer(q, k_c, v_c, k_s, to_groups(v_s), k_w, to_groups(v_w), nsa_gates)

        xc = causal_depthwise_conv(x_rnn, conv_w[l], conv_b[l])
        hr = rg_lru(xc, w_rg_a[l], b_rg_a[l], w_rg_i[l], b_rg_i[l], rg_lambda[l])
        y_rnn = jax.nn.gelu(g_rnn) * hr

        y_x = cross_attention(q_x, mem, g_mem[l], w_mem_kv[l], w_xo[l])

        gm = jax.nn.sigmoid(merge_g).reshape(B, S, N_BRANCHES, D)
        y = gm[:, :, 0] * y_nsa + gm[:, :, 1] * y_rnn + gm[:, :, 2] * y_x
        h = h + y @ w_o[l]

        v = rms_norm(h, g_mlp[l])
        h = h + jnp.square(jax.nn.relu(v @ w_up[l])) @ w_down[l]

    return rms_norm(h, g_final)


def setup_inputs(seed=0):
    out = dict(first_inputs(seed))
    for name, value in second_inputs(seed + 1).items():
        if name != "x":
            out[name + "_2"] = value
    return out


def reference(
    x, mem, ffn1_norm, ffn1_wg, ffn1_wu, ffn1_wd, mix_norm, w_in, a_q_norm, a_k_norm, a_lambda,
    a_sub_norm, b_q_norm, b_k_norm, b_rel_bias, mem_norm, w_mem_kv, c_q_norm, c_k_norm, w_gate,
    b_gate, w_branch, w_out, ffn2_norm, ffn2_wg, ffn2_wu, ffn2_wd, final_norm, mem_2, g_mix_2,
    w_in_2, cmp_pos_k_2, cmp_pos_v_2, w_cmp_k1_2, w_cmp_k2_2, w_cmp_v1_2, w_cmp_v2_2, conv_w_2,
    conv_b_2, w_rg_a_2, b_rg_a_2, w_rg_i_2, b_rg_i_2, rg_lambda_2, g_mem_2, w_mem_kv_2, w_xo_2,
    w_o_2, g_mlp_2, w_up_2, w_down_2, g_final_2,
):
    x = first_block(
        x, mem, ffn1_norm, ffn1_wg, ffn1_wu, ffn1_wd, mix_norm, w_in, a_q_norm, a_k_norm,
        a_lambda, a_sub_norm, b_q_norm, b_k_norm, b_rel_bias, mem_norm, w_mem_kv, c_q_norm,
        c_k_norm, w_gate, b_gate, w_branch, w_out, ffn2_norm, ffn2_wg, ffn2_wu, ffn2_wd,
        final_norm,
    )
    return second_block(
        x, mem_2, g_mix_2, w_in_2, cmp_pos_k_2, cmp_pos_v_2, w_cmp_k1_2, w_cmp_k2_2, w_cmp_v1_2,
        w_cmp_v2_2, conv_w_2, conv_b_2, w_rg_a_2, b_rg_a_2, w_rg_i_2, b_rg_i_2, rg_lambda_2,
        g_mem_2, w_mem_kv_2, w_xo_2, w_o_2, g_mlp_2, w_up_2, w_down_2, g_final_2,
    )


_drawn_inputs = setup_inputs


def setup_inputs(seed=0):
    import zlib

    import numpy as np

    out = dict(_drawn_inputs(seed))
    spreads = {}
    factors = {'mem_2': 8.0,
     'g_mix_2': 8.0,
     'w_in_2': 8.0,
     'cmp_pos_k_2': 8.0,
     'cmp_pos_v_2': 64.0,
     'w_cmp_k1_2': 8.0,
     'w_cmp_k2_2': 8.0,
     'w_cmp_v1_2': 8.0,
     'w_cmp_v2_2': 8.0,
     'conv_w_2': 64.0,
     'conv_b_2': 64.0,
     'w_rg_a_2': 64.0,
     'b_rg_a_2': 64.0,
     'w_rg_i_2': 64.0,
     'b_rg_i_2': 64.0,
     'rg_lambda_2': 64.0,
     'g_mem_2': 8.0,
     'w_mem_kv_2': 8.0,
     'w_xo_2': 8.0,
     'w_o_2': 8.0,
     'g_mlp_2': 64.0,
     'g_final_2': 8.062,
     'w_up_2': 6.456,
     'w_down_2': 5.896}
    for name, (base, spread) in spreads.items():
        noise = np.random.default_rng([zlib.crc32(name.encode()), seed]).standard_normal(out[name].shape)
        drawn = base * np.exp(spread * noise) if base else spread * noise
        out[name] = __import__('jax').numpy.asarray(drawn.astype(out[name].dtype))
    for name, factor in factors.items():
        out[name] = (out[name] * factor).astype(out[name].dtype)
    return out
```

```python
import math
from contextlib import ExitStack

import numpy as np

import concourse.bass as bass
from concourse import mybir

F32 = mybir.dt.float32
F32R = mybir.dt.float32r
ACT = mybir.ActivationFunctionType
ALU = mybir.AluOpType
AX = mybir.AxisListType

P = 128
T = 512
TT = T // P
D = 1024
DC = D // P
MEM = 256
MT = MEM // P
FF = 2816
FF2 = 4096
EPS = 1e-6
NEG = -1e30
CHUNK = 64
NCMP = 31
NC32 = 32
HD = 64
LAMBDA_INIT = 0.8 - 0.6 * math.exp(-0.3 * 0)

VEC_COLS = {}
_at = 0
for _name, _n in (
    ("ffn1_norm", 8), ("mix_norm", 8), ("mem_norm", 8), ("ffn2_norm", 8), ("final_norm", 8),
    ("g_mix", 8), ("g_mem", 8), ("g_mlp", 8), ("g_final", 8),
    ("a_sub", 1), ("b_q", 1), ("b_k", 1), ("c_q", 1), ("c_k", 1),
    ("b_gate", 24), ("conv_w", 32), ("conv_b", 8), ("b_rg_a", 8), ("b_rg_i", 8), ("rg_lambda", 8),
    ("pos_k", 16), ("pos_v", 16), ("lam", 256), ("a_qg", 64), ("a_kg", 64),
):
    VEC_COLS[_name] = (_at, _n)
    _at += _n
NVEC = _at

CST_COLS = {}
_at = 0
for _name, _n in (
    ("ident", 128), ("mask_chunk", 512), ("mask_causal", 512), ("mask_cmp", 128), ("valid", 4),
    ("pads", 4), ("pad_cap", 4),
    ("cosA", 256), ("sinA", 256), ("cosN", 32), ("sinN", 32), ("cosC", 8), ("sinC", 8),
):
    CST_COLS[_name] = (_at, _n)
    _at += _n
NCST = _at


def shape_constants():
    f = np.float32
    out = np.zeros((P, NCST), f)

    def put(name, a):
        at, n = CST_COLS[name]
        out[: a.shape[0], at:at + n] = a.reshape(a.shape[0], n)

    put("ident", np.eye(P, dtype=f))
    p, c = np.arange(P)[:, None], np.arange(P)[None, :]
    chunk, causal = np.zeros((P, T), f), np.zeros((P, T), f)
    chunk[:, T - P:] = np.where(c // CHUNK > p // CHUNK, NEG, 0)
    causal[:, T - P:] = np.where(c > p, NEG, 0)
    put("mask_chunk", chunk)
    put("mask_causal", causal)
    tok = np.arange(T).reshape(TT, P)
    n = np.arange(NC32)
    ok = (16 * n[None, None, :] + 31 <= tok.T[:, :, None]) & (n < NCMP)[None, None, :]
    put("mask_cmp", np.where(ok, 0, NEG).astype(f))
    put("valid", (tok.T >= 31).astype(f))
    put("pads", (T - 1 - tok.T).astype(f))
    put("pad_cap", np.where(tok.T < T - 1, 0, 3e38).astype(f))
    inv = f(10000.0) ** (-np.arange(32, dtype=f) / f(32))
    ang = tok.T[:, :, None].astype(f) * inv
    cos, sin = np.cos(ang).astype(f), np.sin(ang).astype(f)
    put("cosA", np.concatenate([cos, cos], -1))
    put("sinA", np.concatenate([-sin, sin], -1))
    inv2 = f(1.0) / (f(500000.0) ** (np.arange(0, 16, 2, dtype=f) / f(16)))
    ang = tok.T[:, :, None].astype(f) * inv2
    put("cosN", np.cos(ang).astype(f))
    put("sinN", np.sin(ang).astype(f))
    ang = (np.arange(NCMP) * 16 + 31)[:, None].astype(f) * inv2
    put("cosC", np.cos(ang).astype(f))
    put("sinC", np.sin(ang).astype(f))
    return out


def build(nc, a, out):
    ctx = ExitStack()
    with ctx:
        sem = lambda name: ctx.enter_context(nc.semaphore(name))
        top = [16512]
        peak = [0]

        def place(name, shape, dt=F32, at=None):
            size = 4
            for n in shape[1:]:
                size *= n
            off = top[0] if at is None else at
            t = nc.alloc_sbuf_tensor_at(name, shape, dt, offset=off)
            if at is None:
                top[0] += (size + 31) // 32 * 32
                peak[0] = max(peak[0], top[0])
                assert top[0] <= 229344, (name, top[0])
            return t

        xT_at = top[0]
        xT = place("xT", [P, DC, T])
        hH = place("hH", [P, DC, T], F32R)
        hL = place("hL", [P, DC, T], F32R)
        wraw = [place(f"wraw{s}", [P, 2048]) for s in range(2)]
        whi = [place(f"whi{s}", [P, 2048], F32R) for s in range(2)]
        wlo = [place(f"wlo{s}", [P, 2048], F32R) for s in range(2)]
        cst = place("cst", [P, NCST])
        vec = place("vec", [P, NVEC])
        ones = place("ones", [P, P])
        mk_at = top[0]
        mkT = place("mkT", [P, 4, MEM])
        mv = place("mv", [P, MT, 512])
        m2kT = place("m2kT", [P, 2, MEM])
        m2v = place("m2v", [P, MT, 256])
        st = place("st", [P, 96])
        nst = place("nst", [P, 3, TT, 8])
        eps = place("eps", [P, 1])
        gs = place("gs", [P, 8])
        lamw = place("lamw", [P, 8])
        oas = place("oas", [P, 3, 4, TT])
        kcT = place("kcT", [P, 2, NC32])
        vcp = place("vcp", [P, 4, HD])
        norm_at = top[0]
        sqb = [place(f"sqb{s}", [P, T]) for s in range(2)]
        acc = place("acc", [P, T])
        htmp = [place(f"htmp{s}", [P, T]) for s in range(2)]
        diag = place("diag", [P, TT, P])
        arena = top[0]
        S_at = norm_at
        Sm = [place(f"Sm{s}", [P, T], at=S_at + 2048 * s) for s in range(4)]
        Sm.append(place("Sm4", [P, T], at=S_at + 8192))
        bias = place("bias", [P, T], at=S_at + 8192)
        vst = place("vst", [P, TT, P], at=S_at + 10240)
        oa_junk = place("oa_junk", [P, T], at=S_at + 10240)

        def C(name):
            at, n = CST_COLS[name]
            return cst[:, at:at + n]

        def V(name, c=0, n=1):
            at, _ = VEC_COLS[name]
            return vec[:, at + c:at + c + n]

        ident = C("ident")
        memx = [place(f"memx{m}", [P, MT, D]) for m in range(2)]
        mH = [place(f"mH{m}", [P, DC, MEM], F32R) for m in range(2)]
        mL = [place(f"mL{m}", [P, DC, MEM], F32R) for m in range(2)]
        tkM = place("tkM", [P, MT, 512])
        xin = place("xin", [P, TT, D], at=top[0])
        assert top[0] + 16384 <= 229344
        top[0] = arena
        gH = place("gH", [P, 16, T], F32R)
        gL = place("gL", [P, 16, T], F32R)
        act_t = [place(f"act_t{s}", [P, T]) for s in range(2)]
        prod = [place(f"prod{s}", [P, T]) for s in range(2)]
        acc_g = place("acc_g", [P, T])
        prod_junk = place("junk", [P, D], at=norm_at + 4096 + 2048)
        top[0] = arena
        oT = place("oT", [P, 12, T])
        QZ = [place(f"QZ{s}", [P, T]) for s in range(4)]
        bias2 = [bias, place("bias1", [P, T])]
        bias_raw = place("bias_raw", [P, 2, T], at=arena + 8 * 2048)
        PT_at = top[0]
        PT = [place(f"PT{s}", [P, TT, T]) for s in range(2)]
        PTr = place("PTr", [P, 4, 2, T], at=PT_at)
        tk = place("tk", [P, TT, T], at=PT_at)
        rtab = place("rtab", [P, 4, TT, HD], at=PT_at + 8192)
        QT = place("QT", [P, 4, T])
        KT = place("KT", [P, 4, T])
        Vt = place("Vt", [P, TT, 512])
        rt = [place(f"rt{s}", [P, T], at=norm_at + 4096 + 2048 * s) for s in range(2)]
        top[0] = arena + 24576
        oH = [place(f"oH{s}", [P, 4, T], F32R) for s in range(2)]
        oL = [place(f"oL{s}", [P, 4, T], F32R) for s in range(2)]
        y = place("y", [P, DC, T])
        sg = [place(f"sg{s}", [P, T], at=norm_at + 2048 * s) for s in range(2)]
        gt = [place(f"gt{s}", [P, T], at=norm_at + 4096 + 2048 * s) for s in range(2)]
        top[0] = arena
        kcv = place("kcv", [P, 4, T])
        Z = [place(f"Z{s}", [P, 4, T]) for s in range(2)]
        w1c = [place(f"w1c{s}", [P, 16, 256]) for s in range(2)]
        RB = place("RB", [P, 16, 4, NCMP])
        hid = place("hid", [P, 2, 4 * NCMP])
        w2c = place("w2c", [P, 2, 2, HD])
        kct = place("kct", [NCMP, 4, HD])
        crn = place("crn", [NCMP, 4, 4, 8])
        top[0] = arena
        xc = place("xc", [P, DC, T])
        rg = place("rg", [P, DC, T])
        gi = place("gi", [P, DC, T])
        av = place("av", [P, DC, T])
        wrg = [place(f"wrg{s}", [P, DC, P]) for s in range(2)]
        xp = [place(f"xp{s}", [P, T + 4], at=norm_at + 2080 * s) for s in range(2)]
        rt2 = [place(f"rt2{s}", [P, T], at=norm_at + 4160 + 2048 * s) for s in range(2)]
        sp8 = place("sp8", [P, 8, 8], at=norm_at + 8256)
        gg = place("gg", [P, DC, T], at=xT_at)
        sgm = [place(f"sgm{s}", [P, T], at=norm_at + 2080 * s) for s in range(2)]
        yacc = xc
        top[0] = arena + 16384
        QZ2 = [place(f"QZn{s}", [P, T]) for s in range(4)]
        PT2_at = top[0]
        top[0] += 16384
        PTr2 = place("PTnr", [P, 4, 2, T], at=PT2_at)
        tk2 = place("tk2", [P, TT, T], at=PT2_at)
        rn = [place(f"rn{s}", [P, 8, 8], at=PT2_at + 8192 + 256 * s) for s in range(4)]
        kT2 = place("kT2", [P, 4, T])
        yn = place("yn", [P, DC, T])
        PTc = [place("PTc0", [P, T]), place("PTc1", [P, T], at=S_at + 10240)]
        ng = place("ng", [P, TT, 48])
        ngT = place("ngT", [48, T], at=S_at)
        qx = place("qx", [P, 2, T])
        ox = place("ox", [P, 2, T])
        q2 = place("q2", [P, DC, T], at=xT_at)
        v2 = place("v2", [P, TT, 512], at=mk_at)
        top[0] = arena + 16384
        oxH = place("oxH", [P, 2, T], F32R)
        oxL = place("oxL", [P, 2, T], F32R)
        yx = place("yx", [P, DC, T])
        assert top[0] <= arena + 16384 + 8192 + 16384 + 8192

        ps = [ctx.enter_context(nc.psum_tensor(f"ps{b}", [P, T], F32)) for b in range(8)]

        cst_in, x_in = sem("cst_in"), sem("x_in")
        mem_in = [sem(f"mem_in{m}") for m in range(2)]
        w_raw = [sem(f"w_raw{s}") for s in range(2)]
        w_hi = [sem(f"w_hi{s}") for s in range(2)]
        w_lo = [sem(f"w_lo{s}") for s in range(2)]
        slot0_used = sem("slot0_used")
        mm_full = [sem(f"mm_full{b}") for b in range(8)]
        mm_free = [sem(f"mm_free{b}") for b in range(8)]
        pool_cst = sem("pool_cst")
        dve_step, act_step = sem("dve_step"), sem("act_step")
        sq_ready, sq_used = sem("sq_ready"), sem("sq_used")
        stat_full, sd_ready, diag_ready, rr_full = sem("stat_full"), sem("sd_ready"), sem("diag_ready"), sem("rr_full")
        h_tmp, h_hi, h_lo = sem("h_tmp"), sem("h_hi"), sem("h_lo")
        g_hi, g_lo, g_prod = sem("g_hi"), sem("g_lo"), sem("g_prod")
        tok_sq, tok_red, tok_sd, tok_ready = sem("tok_sq"), sem("tok_red"), sem("tok_sd"), sem("tok_ready")
        turn_full, turn_free = sem("turn_full"), sem("turn_free")

        def rows(w):
            return w.rearrange("(c p) n -> p c n", p=P)

        def cols_of(w, base, step, n=256):
            return lambda i: rows(w)[:, :, bass.ds(i * step + base, n)]

        stages = {}
        count = {"k": 0, "b": [0] * 8, "s0": 0}

        def stage(name, its, src, shp, banks, rel):
            stages[name] = dict(its=its, src=src, shp=shp, k0=count["k"], m0=list(count["b"]), rel=rel,
                                s0=count["s0"], name=name)
            count["k"] += its
            for b in banks:
                count["b"][b] += its
            if rel[0] is None:
                count["s0"] += its

        def tok_stage(name, its, w, c0, step=512):
            src = [lambda i, h=h: rows(w)[:, 4 * h:4 * h + 4, bass.ds(i * step + c0, 512)] for h in range(2)]
            n_banks = MT if name in ("mk", "mv", "m2") else TT
            stage(name, its, src, [(4, 512)] * 2, range(n_banks), [None, n_banks - 1])

        def quad_stage(name, its, w, c0, step=512, off=256):
            stage(name, its, [cols_of(w, c0, step), cols_of(w, c0 + off, step)], [(8, 256)] * 2, range(4), [1, 3])

        def down_stage(name, its, w, r0, nk):
            src = [lambda i, s=s: rows(w)[:, r0:r0 + nk, bass.ds(i * 256 + 128 * s, 128)] for s in range(2)]
            stage(name, its, src, [(nk, 128)] * 2, (0, 2), [0, 2])

        def ffn_stages(n, wg, wu, wd):
            for half, (c0, its, nk) in enumerate(((0, 6, 12), (1536, 5, 10))):
                stage(f"up{n}{half}", its, [cols_of(wg, c0, 256), cols_of(wu, c0, 256)], [(8, 256)] * 2, range(4), [1, 3])
                down_stage(f"dn{n}{half}", 4, wd, 12 * half, nk)

        W2 = a["w_in_2"][0]
        tok_stage("mk", 1, a["w_mem_kv"][0], 0)
        tok_stage("mv", 1, a["w_mem_kv"][0], 512)
        tok_stage("m2", 1, a["w_mem_kv_2"][0], 0)
        ffn_stages(1, a["ffn1_wg"][0], a["ffn1_wu"][0], a["ffn1_wd"][0])
        for n, name in enumerate(("aq", "ak", "av", "bq", "bk", "bv", "cq")):
            tok_stage(name, 1, a["w_in"][0], 512 * n)
        for n in range(3):
            wb = a["w_branch"][0, n]
            stage(f"gate{n}", 4, [cols_of(a["w_gate"][0], 1024 * n, 256), cols_of(wb, 0, 256)],
                  [(8, 256), (4, 256)], range(4), [1, 3])
        quad_stage("wo", 2, a["w_out"][0], 0)
        ffn_stages(2, a["ffn2_wg"][0], a["ffn2_wu"][0], a["ffn2_wd"][0])
        quad_stage("kc", 1, W2, 1024)
        quad_stage("gr", 2, W2, 3632)
        quad_stage("xr", 2, W2, 2608)
        quad_stage("m1", 2, W2, 4912 + 1024)
        tok_stage("q", 2, W2, 0)
        tok_stage("ksv", 1, W2, 1536)
        tok_stage("kwv", 1, W2, 2048)
        stage("qx", 1, [cols_of(W2, 4656, 0), cols_of(W2, 2560, 0, 48)], [(8, 256), (8, 48)], range(4), [1, 2])
        quad_stage("m0", 2, W2, 4912)
        stage("xo", 1, [cols_of(a["w_xo_2"][0], 0, 0, 512), cols_of(a["w_xo_2"][0], 512, 0, 512)], [(2, 512)] * 2, range(8), [3, 7])
        quad_stage("m2g", 2, W2, 4912 + 2048)
        quad_stage("wo2", 2, a["w_o_2"][0], 0)
        for half in range(2):
            quad_stage(f"mu{half}", 4, a["w_up_2"][0], 2048 * half)
            down_stage(f"md{half}", 4, a["w_down_2"][0], 16 * half, 16)
        LAST = "md1"

        def loop(eng, n, body):
            if n < 3:
                for i in range(n):
                    body(i)
            else:
                with eng.Fori(0, n) as i:
                    body(i)

        def chunk(t, c):
            return t[:, c, :]

        def f32(ap):
            return ap.bitcast(F32)

        NORMS = ("ffn1", "mix", "ffn2", "final", "g_mix", "g_mlp", "g_final")
        NORM = {n: j for j, n in enumerate(NORMS)}
        HSET = {n: j for j, n in enumerate(("ffn1", "mix", "y1", "ffn2", "g_mix", "y2", "g_mlp"))}
        GAIN = {"ffn1": "ffn1_norm", "mix": "mix_norm", "ffn2": "ffn2_norm", "final": "final_norm",
                "g_mix": "g_mix", "g_mlp": "g_mlp", "g_final": "g_final"}
        G0, at = {}, 0
        for n, c in (("10", 12), ("11", 10), ("20", 12), ("21", 10), ("m0", 16), ("m1", 16)):
            G0[n] = at
            at += c
        PREP, ta, ca = {}, 0, 0
        for n, tiles, chunks in (("mk", MT, 4), ("m2", 0, 2), ("aq", 4, 4), ("ak", 4, 4), ("oa", 0, 4), ("bq", 4, 4),
                                 ("bk", 4, 4), ("cq", 4, 4), ("q0", 4, 4), ("q1", 4, 4), ("kk", 4, 4)):
            PREP[n] = (ta, ca)
            ta, ca = ta + tiles, ca + chunks
        PREP_N = {n: j for j, n in enumerate(("mk", "aq", "ak", "bq", "bk", "cq"))}
        red0, at = {}, 0
        for n, c in (("mk", MT), ("aq", 4), ("ak", 4), ("bq", 4), ("bk", 4), ("cq", 4)):
            red0[n] = at
            at += c

        spill = nc.dram_tensor("residual", (P, DC * T), F32, kind="Internal").ap()
        sp_out, spilled, spill_back = sem("sp_out"), sem("spilled"), sem("spill_back")
        cmp_in, rg_in = sem("cmp_in"), sem("rg_in")
        bias_in = [sem(f"bias_in{h}") for h in range(2)]
        z_in = [sem(f"z_in{m}") for m in range(2)]
        xt_ready, x_turned, mem_norm_ready, mem_lo, mem_turned, mem_hi, mem_sd, mem_sq = (sem(x) for x in (
            "xt_ready", "x_turned", "mem_norm_ready", "mem_lo", "mem_turned", "mem_hi", "mem_sd", "mem_sq"))
        o_hi, o_lo, ox_hi, ox_lo, out_copied, out_turned = (sem(x) for x in ("o_hi", "o_lo", "ox_hi", "ox_lo", "out_copied", "out_turned"))
        cmp_rb, cmp_h, cmp_hid, cmp_o, cmp_copied, cmp_rope, cmp_turn = (sem(x) for x in (
            "cmp_rb", "cmp_h", "cmp_hid", "cmp_o", "cmp_copied", "cmp_rope", "cmp_turn"))
        xp_ready, xc_ready, rg_full, rg_sig, rg_u = (sem(x) for x in ("xp_ready", "xc_ready", "rg_full", "rg_sig", "rg_u"))
        lam_sum, lam_exp, y_done, y1_done, y2_done, merged = (sem(x) for x in ("lam_sum", "lam_exp", "y_done", "y1_done", "y2_done", "merged"))
        xp_zero, sp_in, sp_exp, sp_ready = (sem(x) for x in ("xp_zero", "sp_in", "sp_exp", "sp_ready"))
        rg_a, rg_t, rg_m2, rg_mult = (sem(x) for x in ("rg_a", "rg_t", "rg_m2", "rg_mult"))
        out_ready, acc_zero, qz_zero, vc_done, wrg_zero = (sem(x) for x in ("out_ready", "acc_zero", "qz_zero", "vc_done", "wrg_zero"))
        attn_at = {}
        atc = [0, 0, 0, 0]
        for n, its, steps, turns, maps, groups in (("A", 2, 16, 8, 2, 2), ("B", 4, 8, 8, 4, 1), ("C", 2, 8, 8, 2, 2),
                                                   ("N0", 2, 36, 36, 18, 2), ("N1", 2, 36, 36, 18, 2),
                                                   ("X", 2, 8, 8, 4, 1)):
            staged0 = attn_at[last]["stage0"] + attn_at[last]["its"] if attn_at else 0
            attn_at[n] = dict(its=its, n=steps, S0=atc[0], T0=atc[1], M0=atc[2], O0=atc[3], turns=turns, maps=maps, groups=groups, stage0=staged0)
            last = n
            atc = [atc[0] + its * steps, atc[1] + its * turns, atc[2] + its * maps, atc[3] + its * groups]
        s_full, s_taken, s_masked, s_exp, s_norm = (sem(x) for x in ("s_full", "s_taken", "s_masked", "s_exp", "s_norm"))
        t_full, t_free, pv_done, o_free, staged = (sem(x) for x in ("t_full", "t_free", "pv_done", "o_free", "staged"))
        bias_ready, pair_ready = sem("bias_ready"), sem("pair_ready")
        oa_sq, oa_sd, oa_ready = (sem(x) for x in ("oa_sq", "oa_sd", "oa_ready"))
        for n, per in (("A", 24), ("B", 8), ("C", 8), ("N0", 76), ("N1", 76), ("X", 8)):
            attn_at[n]["order"] = per
        S_RING, T_RING, PV_RING, O_RING = 4, 2, 3, 2

        def load_tile(sp, S, i, s):
            nk, nc_ = S["shp"][s]
            dst = wraw[s][:, 0:nk * nc_].rearrange("p (c n) -> p c n", c=nk)
            sp.dma_start(dst, S["src"][s](i)).then_inc(w_raw[s], 16)

        block = ctx.enter_context(nc.Block())

        @block.sync
        def _(sp):
            for m, name in enumerate(("mem", "mem_2")):
                sp.dma_start(memx[m][:, :, :], a[name][0].rearrange("(m p) d -> p m d", p=P)).then_inc(mem_in[m], 16)
                if m == 0:
                    sp.dma_start(cst[:, :], a["cst"]).then_inc(cst_in, 16)
                    sp.dma_start(vec[:, :], a["vec"]).then_inc(cst_in, 16)
            for h in range(2):
                sp.dma_start(xin[:, 2 * h:2 * h + 2, :],
                             a["x"][0].rearrange("(m p) d -> p m d", p=P)[:, 2 * h:2 * h + 2, :]).then_inc(x_in, 16)
            for S in stages.values():
                def body(i, S=S):
                    for s in range(2):
                        if S["k0"]:
                            sp.wait_ge(w_lo[s], i + S["k0"])
                        load_tile(sp, S, i, s)
                loop(sp, S["its"], body)
            for tt in range(TT):
                sp.wait_ge(out_copied, DC)
                sp.dma_start(out[0, tt * P:(tt + 1) * P, :], xin[:, tt, :]).then_inc(sp_out, 16)
            sp.wait_ge(sp_out, 16 * TT)

        def pool_squares(pool, j, first=False):
            pool.wait_ge(sq_ready, 8 * j + 1)
            pool.memset(acc[:, :], 0.0).then_inc(acc_zero, 1)
            pool.wait_ge(acc_zero, j + 1)
            with pool.Fori(0, DC // 2) as i:
                for s in range(2):
                    pool.wait_ge(sq_ready, i * 2 + (8 * j + s + 1))
                    pool.wait_ge(sq_used, i * 2 + (8 * j + s + 2))
                    pool.tensor_tensor(acc[:, :], acc[:, :], sqb[s][:, :], ALU.add).then_inc(sq_used, 1)

        @block.gpsimd
        def _(pool):
            pool.memset(ones[:, :], 1.0).then_inc(pool_cst, 1)
            pool.memset(eps[:, :], EPS).then_inc(pool_cst, 1)
            pool.memset(kcT[:, :, :], 0.0).then_inc(pool_cst, 1)
            pool.memset(vcp[:, :, :], 0.0).then_inc(pool_cst, 1)
            pool.memset(diag[:, 0, 0:2], 0.0).then_inc(sq_used, 2)
            pool_squares(pool, 0)
            pool_squares(pool, 1)
            for z in range(4):
                half = slice(64, 128) if z % 2 == 0 else slice(0, 64)
                pool.wait_ge(sq_used, 2 + 16) if z == 0 else pool.wait_ge(qz_zero, z)
                pool.memset(QZ[z][half, :], 0.0).then_inc(qz_zero, 1)
            for h in range(8 + 2):
                if h >= 2:
                    b = bias2[h % 2]
                    if h < 4:
                        pool.wait_ge(o_free, O_RING + attn_at["B"]["O0"])
                    else:
                        pool.wait_ge(s_masked, attn_at["B"]["S0"] + 8 * ((h - 2) // 2))
                    pool.wait_ge(bias_in[h % 2], 16 * (h // 2))
                    pool.tensor_tensor(b[:, :], bias_raw[:, h % 2, :], C("mask_chunk"), ALU.add).then_inc(bias_ready, 1)
                if h < 8:
                    if h >= 2:
                        pool.wait_ge(bias_ready, h - 1)
                    pool.dma_start(bias_raw[:, h % 2, :], a["rel"][h]).then_inc(bias_in[h % 2], 16)
            pool_squares(pool, NORM["ffn2"])
            pool.wait_ge(sq_ready, 8 * NORM["final"] + 1)
            for m, a_ in enumerate((acc, acc_g)):
                pool.memset(a_[:, :], 0.0).then_inc(acc_zero, 1)
                pool.wait_ge(acc_zero, NORM["final"] + 1 + m)
            with pool.Fori(0, DC) as i:
                for s, a_ in enumerate((acc, acc_g)):
                    pool.wait_ge(sq_ready, i * 2 + (8 * NORM["final"] + s + 1))
                    pool.wait_ge(sq_used, i * 2 + (8 * NORM["final"] + s + 2))
                    pool.tensor_tensor(a_[:, :], a_[:, :], sqb[s][:, :], ALU.add).then_inc(sq_used, 1)
            pool.wait_ge(h_tmp, 8 * (NORM["g_mix"] + 1))
            pool.dma_start(spill, xT[:, :, :].rearrange("p c t -> p (c t)")).then_inc(spilled, 16)
            for m, n in enumerate("kv"):
                pool.dma_start(w1c[m][:, :, :], a[f"w_cmp_{n}1_2"][0].rearrange("(m p) n -> p m n", p=P)).then_inc(cmp_in, 16)
                pool.dma_start(w2c[:, m, :, :], a[f"w_cmp_{n}2_2"][0].rearrange("(c p) n -> p c n", p=P)).then_inc(cmp_in, 16)
            for m in range(2):
                for g in range(4):
                    pool.wait_ge(mm_free[2 * m + g // 2], 1 + stages["kc"]["m0"][2 * m + g // 2] + 1)
                    src = kcv[64 * (g % 2):64 * (g % 2) + 64, 2 * m + g // 2, :]
                    pool.dma_start(Z[m][0:64, g, :], src).then_inc(z_in[m], 16)
                    pool.dma_start(Z[m][64:128, g, 0:T - 1], src[:, 1:T]).then_inc(z_in[m], 16)
            pool.wait_ge(vc_done, 1)
            for m in range(2):
                pool.memset(wrg[m][:, :, :], 0.0).then_inc(wrg_zero, 1)
            pool.wait_ge(wrg_zero, 2)
            for m, n in enumerate("ai"):
                w = a[f"w_rg_{n}_2"][0].rearrange("(c b) i j -> b i c j", b=2)
                for b in range(2):
                    pool.dma_start(wrg[m][64 * b:64 * b + 64, :, 64 * b:64 * b + 64], w[b]).then_inc(rg_in, 16)
            pool.wait_ge(y1_done, DC)
            for z in range(4):
                half = slice(64, 128) if z < 2 else slice(0, 64)
                pool.wait_ge(qz_zero, 4 + z)
                pool.memset(QZ2[z][half, :], 0.0).then_inc(qz_zero, 1)
            for h in range(2):
                pool.wait_ge(qz_zero, 8 + h)
                pool.memset(PTc[h][:, :], 0.0).then_inc(qz_zero, 1)
            pool.wait_ge(pv_done, PV_RING + attn_at["X"]["M0"])
            pool.wait_ge(spilled, 16)
            pool.dma_start(xT[:, :, :].rearrange("p c t -> p (c t)"), spill).then_inc(spill_back, 16)
            pool_squares(pool, NORM["g_mlp"])
            pool_squares(pool, NORM["g_final"])

        class Order:

            def __init__(self, eng, sem_):
                self.eng, self.sem, self.n, self.i, self.per = eng, sem_, 0, None, 0

            def __call__(self, ins):
                ins.then_inc(self.sem, 1)
                self.n += 1
                self.eng.wait_ge(self.sem, self.n if self.i is None else self.i * self.per + self.n)

            def loop(self, n, per, body):
                if n < 3:
                    for i in range(n):
                        at = self.n
                        body(i)
                        assert self.n == at + per, (self.n - at, per)
                else:
                    at = self.n
                    with self.eng.Fori(0, n) as i:
                        self.i, self.per = i, per
                        body(i)
                        assert self.n == at + per, (self.n - at, per)
                    self.i, self.n = None, at + n * per

        def full(S, b, i):
            return i + (S["m0"][b] + 1)

        def free_before(S, b, i):
            return i + (S["m0"][b] + 1)

        def free_after(S, b, i):
            return i + (S["m0"][b] + 2)

        def act_split(act, S, s, i):
            if S["name"] == LAST and isinstance(i, int) and i == S["its"] - 1:
                return
            act.wait_ge(w_raw[s], i * 16 + 16 * (S["k0"] + 2))
            if S["rel"][s] is None:
                act.wait_ge(slot0_used, i + (S["s0"] + 1))
            else:
                act.wait_ge(mm_full[S["rel"][s]], full(S, S["rel"][s], i))
            act.activation(whi[s][:, :], wraw[s][:, :], ACT.Copy).then_inc(w_hi[s], 1)

        def dve_split(dve, S, s, i):
            if S["name"] == LAST and isinstance(i, int) and i == S["its"] - 1:
                return
            dve.wait_ge(w_hi[s], i + (S["k0"] + 2))
            dve.tensor_tensor(wlo[s][:, :], wraw[s][:, :], f32(whi[s][:, :]), ALU.subtract).then_inc(w_lo[s], 1)

        def paired(kind):
            return kind in "BNX"

        def step_of(kind, t):
            if kind == "A":
                return t // 8, t % 2, (t % 8) // 2
            if kind == "N":
                pair, x = t // 18, (t % 18) // 2
                return 2 * pair + t % 2, "c" if x == 0 else "s" if x < 5 else "w", (x - 1) % 4 if x else 0
            if kind == "C":
                return t // 4, 0, t % 4
            return t % 2, 0, t // 2

        def lag_of(kind):
            return 4 if kind in "ANX" else 3

        def S_of(kind, t):
            return Sm[t % (lag_of(kind) + 1)]

        def width(kind, m, qt):
            if m == "c":
                return 4 * NC32
            return MEM if kind in ("C", "X") else P * (qt + 1)

        def turned(kind, t):
            return kind != "A" or t % 2 == 1

        def turn_no(kind, t):
            return t // 2 if kind == "A" else t

        def last_of_map(kind, t):
            if kind == "A":
                return t // 8 if t % 8 == 7 else None
            if kind == "C":
                return t // 4 if t % 4 == 3 else None
            return t // 2 if t % 2 == 1 else None

        def pt_of(kind, m):
            if not paired(kind):
                return PT[m % 2]
            if kind == "N" and m % 9 == 0:
                return PTc
            ring = PTr if kind == "B" else PTr2
            return [ring[:, m % 4, h, :] for h in range(2)]

        def group_of(kind, m):
            return m if kind in ("A", "C") else m // 9 if kind == "N" else 0

        def pt_free(A, kind, i, m):
            if not paired(kind):
                return M_(A, i, m) + (PV_RING - 1)
            if m < 4:
                return M_(A, i, 0) + PV_RING
            return M_(A, i, m) + (PV_RING - 3)

        def S_(A, i, t):
            return i * A["n"] + (A["S0"] + t)

        def T_(A, i, u):
            return i * A["turns"] + (A["T0"] + u)

        def M_(A, i, m):
            return i * A["maps"] + (A["M0"] + m)

        def O_(A, i, g):
            return i * A["groups"] + (A["O0"] + g)

        def pe_attention(pe, name, q_of, k_of, v_of):
            kind = name[0]
            A = attn_at[name]
            lag = lag_of(kind)
            stage0 = A["stage0"]

            def body(i):
                pe.wait_ge(staged, i + (stage0 + 1))
                for slot in range(A["n"] + lag):
                    if slot < A["n"]:
                        t = slot
                        h, m, qt = step_of(kind, t)
                        bank = ps[4 + t % 4]
                        pe.wait_ge(s_masked, S_(A, i, t) + (1 - S_RING)) if not (isinstance(i, int) and S_(A, i, t) < S_RING) else None
                        if m == "c":
                            for q in range(TT):
                                mm = pe.matmul(bank[:, q * NC32:(q + 1) * NC32], q_of(i, h, m, q), k_of(i, h, m, NC32), start=True, stop=True)
                        else:
                            n = width(kind, m, qt)
                            mm = pe.matmul(bank[:, 0:n], q_of(i, h, m, qt), k_of(i, h, m, n), start=True, stop=True)
                        mm.then_inc(s_full, 1)
                    t = slot - lag
                    if t >= 0 and turned(kind, t):
                        h, m, qt = step_of(kind, t)
                        u = turn_no(kind, t)
                        bank = ps[u % 2]
                        pe.wait_ge(s_norm, S_(A, i, t) + 1)
                        pe.wait_ge(t_free, T_(A, i, u) + 1)
                        if m == "c":
                            for q in range(TT):
                                mm = pe.transpose(bank[0:NC32, q * P:(q + 1) * P], S_of(kind, t)[:, q * NC32:(q + 1) * NC32], ident)
                        else:
                            for kc in range(width(kind, m, qt) // P):
                                mm = pe.transpose(bank[:, kc * P:(kc + 1) * P], S_of(kind, t)[:, kc * P:(kc + 1) * P], ident)
                        mm.then_inc(t_full, 1)
                    for te in ((t - 2, t - 1, t) if t == A["n"] - 1 else (t - 2,)):
                        m = last_of_map(kind, te) if te >= 0 else None
                        if m is None:
                            continue
                        g = group_of(kind, m)
                        u = turn_no(kind, te)
                        pe.wait_ge(t_free, T_(A, i, u) + (T_RING + 1))
                        if A["groups"] == 1:
                            if m == 0:
                                pe.wait_ge(o_free, O_(A, i, g) + O_RING)
                        elif kind != "N" or m % 9 == 0:
                            pe.wait_ge(o_free, O_(A, i, g) + 1)
                        obank = ps[2 + g % 2]
                        src = pt_of(kind, m)
                        mm = v_of(i, m, src, obank)
                        mm.then_inc(pv_done, 1)
            loop(pe, A["its"], body)

        def act_attention(act, name, o_to):
            kind = name[0]
            A = attn_at[name]
            lag = lag_of(kind)

            def body(i):
                for slot in range(A["n"] + lag - 1):
                    if slot < A["n"]:
                        t = slot
                        h, m, qt = step_of(kind, t)
                        n = width(kind, m, qt)
                        act.wait_ge(s_masked, S_(A, i, t) + 1)
                        if m == "c":
                            act.activation(S_of(kind, t)[:, 0:n], S_of(kind, t)[:, 0:n], ACT.Exp).then_inc(s_exp, 1)
                        else:
                            if m == "w":
                                at = (52 if qt == TT - 1 else 8) + t % 4
                                act.activation(st[:, 48 + t % 4:49 + t % 4], st[:, at:at + 1], ACT.Exp)
                            act.activation(S_of(kind, t)[:, 0:n], S_of(kind, t)[:, 0:n], ACT.Exp, bias=st[:, 8 + t % 4:9 + t % 4],
                                           scale=-1.0, accum_out=st[:, 12 + t % 4:13 + t % 4]).then_inc(s_exp, 1)
                    t = slot - (lag - 1)
                    if t >= 0 and turned(kind, t):
                        h, m, qt = step_of(kind, t)
                        u = turn_no(kind, t)
                        bank = ps[u % 2]
                        te = next(x for x in range(t, A["n"]) if last_of_map(kind, x) is not None)
                        mp = last_of_map(kind, te)
                        dst = pt_of(kind, mp)
                        if paired(kind):
                            dst = dst[t % 2]
                        act.wait_ge(t_full, T_(A, i, u) + 1)
                        act.wait_ge(pv_done, pt_free(A, kind, i, mp))
                        if m == "c":
                            act.activation(dst[0:NC32, :], bank[0:NC32, :], ACT.Copy).then_inc(t_free, 1)
                        else:
                            nk = width(kind, m, qt) // P
                            if paired(kind):
                                act.activation(dst[:, 0:nk * P], bank[:, 0:nk * P], ACT.Copy).then_inc(t_free, 1)
                                nk = 0
                        if m != "c" and nk:
                            act.activation(dst[:, 0:nk, qt * P:(qt + 1) * P], bank[:, 0:nk * P].rearrange("p (c q) -> p c q", c=nk),
                                           ACT.Copy).then_inc(t_free, 1)
                    if t >= 0:
                        for te in ((t - 4, t - 3, t - 2, t - 1, t) if t == A["n"] - 1 else (t - 4,)):
                            mp = last_of_map(kind, te) if te >= 0 else None
                            if mp is None:
                                continue
                            g = group_of(kind, mp)
                            if kind == "A":
                                act.wait_ge(pv_done, M_(A, i, mp) + (PV_RING + 1))
                                head = 2 * i + g
                                if head:
                                    act.wait_ge(oa_sq, head)
                                for q in range(TT):
                                    sq = act.activation(oa_junk[:, q * P:(q + 1) * P], ps[2 + g][:, q * P:(q + 1) * P], ACT.Square,
                                                        accum_out=oas[:, 0, head, q:q + 1])
                                sq.then_inc(oa_sq, 1)
                                act.activation(oT[:, head, :], ps[2 + g][:, :], ACT.Copy).then_inc(o_free, 1)
                            if kind == "C" or (kind == "N" and mp % 9 == 8) or (kind in "BX" and mp == 3):
                                act.wait_ge(pv_done, M_(A, i, mp) + (PV_RING + 1))
                                act.activation(o_to(i, g), ps[2 + g % 2][:, :], ACT.Copy).then_inc(o_free, 1)
            loop(act, A["its"], body)

        def dve_attention(dve, order, name, stage_in, mask_of, gate_of=None):
            kind = name[0]
            A = attn_at[name]

            def body(i):
                stage_in(i)
                for slot in range(A["n"] + 1):
                    if slot < A["n"]:
                        t = slot
                        h, m, qt = step_of(kind, t)
                        n = width(kind, m, qt)
                        s_ = S_of(kind, t)
                        dve.wait_ge(s_full, S_(A, i, t) + 1)
                        if m == "c":
                            order(dve.tensor_tensor(s_[:, 0:n], ps[4 + t % 4][:, 0:n], C("mask_cmp"), ALU.add))
                            v = s_[:, 0:n].rearrange("p (q k) -> p q k", q=TT)
                            order(dve.tensor_reduce(st[:, 32:36], v, AX.X, ALU.max))
                            dve.tensor_tensor(v, v, st[:, 32:36].unsqueeze(2).broadcast_to([P, TT, NC32]), ALU.subtract).then_inc(s_masked, 1)
                        else:
                            if kind == "B" and qt == 0:
                                dve.wait_ge(bias_ready, i * 2 + (h + 1))
                            dve.sem_inc(s_taken, 1)
                            neg_max = st[:, 8 + t % 4:9 + t % 4]
                            scored = dve.tensor_tensor_reduce(s_[:, 0:n], ps[4 + t % 4][:, 0:n], mask_of(t, n), -1.0,
                                                              0.0 if m == "w" and qt < TT - 1 else 3e38, ALU.add, ALU.min, neg_max)
                            if m == "w" and qt == TT - 1:
                                order(scored)
                                order(dve.tensor_scalar(st[:, 52 + t % 4:53 + t % 4], neg_max, 0.0, None, ALU.min))
                                scored = dve.tensor_tensor(neg_max, neg_max, C("pad_cap")[:, qt:qt + 1], ALU.min)
                            scored.then_inc(s_masked, 1)
                    t = slot - 1
                    if t >= 0:
                        h, m, qt = step_of(kind, t)
                        n = width(kind, m, qt)
                        s_ = S_of(kind, t)
                        c = t % 4
                        dve.wait_ge(s_exp, S_(A, i, t) + 1)
                        if m == "c":
                            v = s_[:, 0:n].rearrange("p (q k) -> p q k", q=TT)
                            order(dve.tensor_reduce(st[:, 36:40], v, AX.X, ALU.add))
                            order(dve.reciprocal(st[:, 40:44], st[:, 36:40]))
                            order(dve.tensor_tensor(st[:, 44:48], st[:, 40:44], gate_of(i, h, m, None), ALU.mult))
                            dve.tensor_tensor(v, v, st[:, 44:48].unsqueeze(2).broadcast_to([P, TT, NC32]), ALU.mult).then_inc(s_norm, 1)
                        else:
                            if m == "w":
                                order(dve.scalar_tensor_tensor(st[:, 12 + c:13 + c], st[:, 48 + c:49 + c], C("pads")[:, qt:qt + 1],
                                                               st[:, 12 + c:13 + c], ALU.mult, ALU.add))
                            order(dve.reciprocal(st[:, 16 + c:17 + c], st[:, 12 + c:13 + c]))
                            if kind == "A" and m == 1:
                                order(dve.tensor_tensor(st[:, 16 + c:17 + c], st[:, 16 + c:17 + c], gs[:, 3:4], ALU.mult))
                                dve.scalar_tensor_tensor(s_[:, 0:n], s_[:, 0:n], st[:, 16 + c:17 + c], S_of(kind, t - 1)[:, 0:n],
                                                         ALU.mult, ALU.add).then_inc(s_norm, 1)
                            elif kind == "N":
                                dve.tensor_scalar(s_[:, 0:n], s_[:, 0:n], st[:, 16 + c:17 + c], gate_of(i, h, m, qt),
                                                  ALU.mult, ALU.mult).then_inc(s_norm, 1)
                            else:
                                dve.tensor_scalar(s_[:, 0:n], s_[:, 0:n], st[:, 16 + c:17 + c], None, ALU.mult).then_inc(s_norm, 1)
                                if kind == "A":
                                    dve.wait_ge(s_norm, S_(A, i, t) + 1)
            order.loop(A["its"], A["order"], body)

        def attention_over(eng, name):
            A = attn_at[name]
            eng.wait_ge(t_free, T_RING + A["T0"] + A["its"] * A["turns"])
            eng.wait_ge(o_free, O_RING + A["O0"] + A["its"] * A["groups"])

        def mm3(pe, o, lh, ll, rh, rl, start, stop):
            pe.matmul(o, lh, rh, start=start, stop=False)
            pe.matmul(o, lh, rl, start=False, stop=False)
            return pe.matmul(o, ll, rh, start=False, stop=stop)

        def pe_cols(pe, S, banks, rh, rl, ready, n=T, fresh=False):
            def body(i, chunks_outside=False):
                for s in range(2):
                    nk, nc_ = S["shp"][s]
                    pe.wait_ge(w_lo[s], i + (S["k0"] + 1))

                    def product(g, b, kc):
                        at = kc * nc_ + g * P
                        return mm3(pe, ps[b][:, 0:n], whi[s][:, at:at + P], wlo[s][:, at:at + P],
                                   rh(i, s, kc), rl(i, s, kc), kc == 0, kc == nk - 1)
                    if chunks_outside and s == 0:
                        for b in banks[s]:
                            pe.wait_ge(mm_free[b], free_before(S, b, i))
                        for kc in range(nk):
                            ready(pe, s, kc)
                            for g, b in enumerate(banks[s]):
                                mm = product(g, b, kc)
                                if kc == nk - 1:
                                    mm.then_inc(mm_full[b], 1)
                        continue
                    for g, b in enumerate(banks[s]):
                        pe.wait_ge(mm_free[b], free_before(S, b, i))
                        for kc in range(nk):
                            if g == 0:
                                ready(pe, s, kc)
                            mm = product(g, b, kc)
                        mm.then_inc(mm_full[b], 1)
            if fresh:
                body(0, True)
                if S["its"] < 4:
                    for i in range(1, S["its"]):
                        body(i)
                else:
                    with pe.Fori(1, S["its"]) as i:
                        body(i)
            else:
                loop(pe, S["its"], body)

        def pe_toks(pe, S, i, lh, ll, ready, tiles=TT, fresh=False):
            for s in range(2):
                pe.wait_ge(w_lo[s], i + (S["k0"] + 1))
                outside = fresh and s == 0
                for n in range(4 * tiles):
                    k, t = (n // tiles, n % tiles) if outside else (n % 4, n // 4)
                    if s == 0 and k == 0:
                        pe.wait_ge(mm_free[t], free_before(S, t, i))
                    kc = 4 * s + k
                    if t == 0:
                        ready(pe, s, kc)
                    a_, b_ = lh[:, kc, t * P:(t + 1) * P], ll[:, kc, t * P:(t + 1) * P]
                    wh, wl = whi[s][:, k * 512:(k + 1) * 512], wlo[s][:, k * 512:(k + 1) * 512]
                    mm = mm3(pe, ps[t][:, :], a_, b_, wh, wl, kc == 0, kc == 7)
                    if kc == 7:
                        mm.then_inc(mm_full[t], 1)
                if s == 0:
                    mm.then_inc(slot0_used, 1)

        def pe_norm(pe, name):
            j = NORM[name]
            pe.wait_ge(sq_used, 2 + 8 * (j + 1))
            for q in range(TT):
                mm = pe.matmul(ps[4][:, q:q + 1], acc[:, q * P:(q + 1) * P], ones[:, 0:1], start=True, stop=True)
            mm.then_inc(stat_full, 1)
            pe.wait_ge(diag_ready, j + 1)
            pe.matmul(ps[5][:, :], ones[:, :], diag[:, :, :].rearrange("p a b -> p (a b)"), start=True, stop=True).then_inc(rr_full, 1)

        def pe_norm_pair(pe):
            j = NORM["g_mix"]
            pe.wait_ge(sq_used, 2 + 8 * (j + 1))
            for m, a_ in enumerate((acc, acc_g)):
                for q in range(TT):
                    mm = pe.matmul(ps[4 + 3 * m][:, q:q + 1], a_[:, q * P:(q + 1) * P], ones[:, 0:1], start=True, stop=True)
                mm.then_inc(stat_full, 1)
            for m in range(2):
                pe.wait_ge(diag_ready, j + m)
                pe.matmul(ps[5 + m][:, :], ones[:, :], diag[:, :, :].rearrange("p a b -> p (a b)"), start=True, stop=True).then_inc(rr_full, 1)

        def pe_turn(pe, name, cols, nchunks, tiles=TT, src=None):
            t0, c0 = PREP[name]
            if name == "m2":
                pe.wait_ge(mm_free[1], free_after(stages["m2"], 1, 0))
            elif name == "oa":
                pe.wait_ge(oa_ready, 4)
            else:
                pe.wait_ge(tok_ready, t0 + tiles)
            for c in range(nchunks):
                if c0 + c >= 4:
                    pe.wait_ge(turn_free, c0 + c - 3)
                for t in range(tiles):
                    mm = pe.transpose(ps[4 + (c0 + c) % 4][:, t * P:(t + 1) * P], cols(t, c), ident)
                mm.then_inc(turn_full, 1)

        def hset_ready(name):
            j = HSET[name]

            def ready(pe, s, kc):
                if s == 0 or kc >= 4:
                    pe.wait_ge(h_lo, 8 * j + kc + 1)
            return ready

        def gready(key):
            def ready(pe, s, kc):
                if s == 0:
                    pe.wait_ge(g_lo, G0[key] + kc + 1)
            return ready

        def no_wait(pe, s, kc):
            pass

        hh = lambda i, s, kc: hH[:, kc, :]
        hl = lambda i, s, kc: hL[:, kc, :]
        gh = lambda i, s, kc: gH[:, kc, :]
        gl = lambda i, s, kc: gL[:, kc, :]
        QUAD = [(0, 1), (2, 3)]
        mem_cols = lambda t, c: tkM[:, t, c * P:(c + 1) * P]
        tk_cols = lambda t, c: tk[:, t, c * P:(c + 1) * P]
        k2_cols = lambda t, c: tk2[:, t, c * P:(c + 1) * P]

        def pe_ffn(pe, n, name):
            for half in range(2):
                pe_cols(pe, stages[f"up{n}{half}"], QUAD, hh, hl, hset_ready(name), fresh=half == 0)
                pe_cols(pe, stages[f"dn{n}{half}"], [(0,), (2,)], gh, gl, gready(f"{n}{half}"))

        def pv_a(i, m, src, ob):
            for q in range(TT):
                for kc in range(q + 1):
                    mm = nc.tensor.matmul(ob[:, q * P:(q + 1) * P], src[:, kc, q * P:(q + 1) * P],
                                          Vt[:, kc, bass.ds((i * 2 + m) * P, P)], start=kc == 0, stop=kc == q)
            return mm

        def pv_pair(ob, qt, nk, val, src, start=True, stop=True):
            for kc in range(nk):
                for h in range(2):
                    mm = nc.tensor.matmul(ob[HD * h:HD * h + HD, qt * P:(qt + 1) * P], val(h, kc), src[h][:, kc * P:(kc + 1) * P],
                                          start=start and kc == 0, stop=stop and kc == nk - 1)
            return mm

        def pv_b(i, m, src, ob):
            return pv_pair(ob, m, m + 1, lambda h, kc: vst[:, kc, HD * h:HD * h + HD], src)

        def pv_c(i, m, src, ob):
            for kc in range(MT):
                mm = nc.tensor.matmul(ob[:, :], vst[:, 2 * m + kc, :], src[:, kc, :], start=kc == 0, stop=kc == MT - 1)
            return mm

        def pv_x(i, m, src, ob):
            return pv_pair(ob, m, MT, lambda h, kc: m2v[:, kc, (2 * i + h) * HD:(2 * i + h + 1) * HD], src)

        def pv_n(aa):
            def pv(i, m, src, ob):
                g, x = 2 * aa + m // 9, m % 9
                if x == 0:
                    for h in range(2):
                        mm = nc.tensor.matmul(ob[HD * h:HD * h + HD, :], vcp[:, g, :], src[h][:, :], start=True, stop=False)
                    return mm
                qt = (x - 1) % 4
                at = (256 if x >= 5 else 0) + g * HD
                return pv_pair(ob, qt, qt + 1, lambda h, kc: v2[:, kc, at:at + HD], src, start=False, stop=x == 8)
            return pv

        def pe_compress(pe):
            pe.wait_ge(cmp_in, 64)
            for m in range(2):
                for hc in range(2):
                    for k in range(16):
                        if hc == 0:
                            pe.wait_ge(cmp_rb, 16 * m + k + 1)
                        mm = pe.matmul(ps[4 + hc][:, 0:4 * NCMP], w1c[m][:, k, hc * P:(hc + 1) * P],
                                       RB[:, k, :, :].rearrange("p g n -> p (g n)"), start=k == 0, stop=k == 15)
                    mm.then_inc(cmp_h, 1)
                pe.wait_ge(cmp_hid, 2 * m + 2)
                for g in range(4):
                    for hc in range(2):
                        mm = pe.matmul(ps[6 + m][0:NCMP, g * HD:(g + 1) * HD], hid[:, hc, g * NCMP:(g + 1) * NCMP],
                                       w2c[:, m, hc, :], start=hc == 0, stop=hc == 1)
                mm.then_inc(cmp_o, 1)
            pe.wait_ge(cmp_rope, 1)
            for aa in range(2):
                mm = pe.transpose(ps[6][:, 256 + aa * NC32:256 + aa * NC32 + NCMP],
                                  kct[:, 2 * aa:2 * aa + 2, :].rearrange("p g d -> p (g d)"), ident[0:NCMP, 0:NCMP])
            mm.then_inc(cmp_turn, 1)

        def pe_rg(pe):
            pe.wait_ge(rg_in, 64)
            for c in range(DC):
                pe.wait_ge(xc_ready, c + 1)
                if c >= 2:
                    pe.wait_ge(rg_sig, 2 * (c - 1))
                for m in range(2):
                    pe.matmul(ps[4 + 2 * (c % 2) + m][:, :], wrg[m][:, c, :], xc[:, c, :], start=True, stop=True).then_inc(rg_full, 1)

        @block.tensor
        def _(pe):
            pe.wait_ge(cst_in, 32)
            pe.wait_ge(x_in, 32)
            for c in range(DC):
                if c >= 2:
                    pe.wait_ge(xt_ready, c - 1)
                for t in range(TT):
                    mm = pe.transpose(ps[6 + c % 2][:, t * P:(t + 1) * P], xin[:, t, c * P:(c + 1) * P], ident)
                mm.then_inc(x_turned, 1)
            for m in range(2):
                pe.wait_ge(mem_norm_ready, m + 1)
                for c in range(0, DC, 2):
                    n = 4 * m + c // 2
                    if n >= 4:
                        pe.wait_ge(mem_lo, 2 * (n - 3))
                    for d in range(2):
                        for t in range(MT):
                            mm = pe.transpose(ps[n % 4][:, (2 * d + t) * P:(2 * d + t + 1) * P],
                                              memx[m][:, t, (c + d) * P:(c + d + 1) * P], ident)
                    mm.then_inc(mem_turned, 1)

            def mem_ready(m):
                def ready(pe_, s, kc):
                    pe_.wait_ge(mem_lo, 8 * m + kc + 1)
                return ready
            pe.wait_ge(mem_lo, 16)
            pe_toks(pe, stages["mk"], 0, mH[0], mL[0], mem_ready(0), MT, fresh=True)
            pe_toks(pe, stages["mv"], 0, mH[0], mL[0], no_wait, MT)
            pe_turn(pe, "mk", mem_cols, 4, MT)
            pe_toks(pe, stages["m2"], 0, mH[1], mL[1], no_wait, MT)
            pe_turn(pe, "m2", mem_cols, 2, MT)
            pe.wait_ge(turn_free, 6)
            pe_norm(pe, "ffn1")
            pe_ffn(pe, 1, "ffn1")
            pe_norm(pe, "mix")
            pe_toks(pe, stages["aq"], 0, hH, hL, hset_ready("mix"), fresh=True)
            pe_toks(pe, stages["ak"], 0, hH, hL, no_wait)
            pe_turn(pe, "aq", tk_cols, 4)
            pe_toks(pe, stages["av"], 0, hH, hL, no_wait)
            pe_turn(pe, "ak", tk_cols, 4)
            pe_attention(pe, "A", lambda i, h, m, q: QZ[2 * h + m][:, q * P:(q + 1) * P],
                         lambda i, h, m, n: KT[:, i * 2 + h, 0:n], pv_a)
            attention_over(pe, "A")
            pe_toks(pe, stages["bq"], 0, hH, hL, no_wait)
            pe_turn(pe, "oa", lambda t, c: oT[:, c, t * P:(t + 1) * P], 4)
            pe_toks(pe, stages["bk"], 0, hH, hL, no_wait)
            pe_turn(pe, "bq", tk_cols, 4)
            pe_toks(pe, stages["bv"], 0, hH, hL, no_wait)
            pe_turn(pe, "bk", tk_cols, 4)
            pe_attention(pe, "B", lambda i, h, m, q: QZ[h][:, q * P:(q + 1) * P],
                         lambda i, h, m, n: KT[:, i, 0:n], pv_b)
            attention_over(pe, "B")
            pe_toks(pe, stages["cq"], 0, hH, hL, no_wait)
            pe_turn(pe, "cq", tk_cols, 4)
            pe_attention(pe, "C", lambda i, h, m, q: QZ[h][:, q * P:(q + 1) * P],
                         lambda i, h, m, n: mkT[:, i * 2 + h, :], pv_c)
            attention_over(pe, "C")
            for n in range(3):
                def ready(pe_, s, kc, n=n):
                    if s == 1:
                        pe_.wait_ge(o_lo, 4 * n + kc + 1)
                pe_cols(pe, stages[f"gate{n}"], QUAD,
                        lambda i, s, kc, n=n: hH[:, kc, :] if s == 0 else oH[n % 2][:, kc, :],
                        lambda i, s, kc, n=n: hL[:, kc, :] if s == 0 else oL[n % 2][:, kc, :], ready)
            pe_cols(pe, stages["wo"], QUAD, hh, hl, hset_ready("y1"), fresh=True)
            pe_norm(pe, "ffn2")
            pe_ffn(pe, 2, "ffn2")
            pe_norm_pair(pe)
            pe_cols(pe, stages["kc"], QUAD, hh, hl, hset_ready("g_mix"), fresh=True)
            pe_cols(pe, stages["gr"], QUAD, hh, hl, no_wait)
            pe_compress(pe)
            pe_cols(pe, stages["xr"], QUAD, hh, hl, no_wait)
            pe_rg(pe)
            pe_cols(pe, stages["m1"], QUAD, hh, hl, no_wait)
            for n in range(2):
                pe_toks(pe, stages["q"], n, hH, hL, no_wait)
                if n:
                    pe_turn(pe, "q0", k2_cols, 4)
            pe_toks(pe, stages["ksv"], 0, hH, hL, no_wait)
            pe_turn(pe, "q1", k2_cols, 4)
            pe_toks(pe, stages["kwv"], 0, hH, hL, no_wait)
            S = stages["qx"]
            pe.wait_ge(w_lo[0], S["k0"] + 1)
            for g in range(2):
                pe.wait_ge(mm_free[g], free_before(S, g, 0))
                for kc in range(DC):
                    at = kc * 256 + g * P
                    mm = mm3(pe, ps[g][:, :], whi[0][:, at:at + P], wlo[0][:, at:at + P], hH[:, kc, :], hL[:, kc, :], kc == 0, kc == 7)
                mm.then_inc(mm_full[g], 1)
            pe.wait_ge(w_lo[1], S["k0"] + 1)
            pe.wait_ge(mm_free[2], free_before(S, 2, 0))
            for kc in range(DC):
                mm = mm3(pe, ps[2][0:48, :], whi[1][:, kc * 48:(kc + 1) * 48], wlo[1][:, kc * 48:(kc + 1) * 48],
                         hH[:, kc, :], hL[:, kc, :], kc == 0, kc == 7)
            mm.then_inc(mm_full[2], 1)
            pe_turn(pe, "kk", k2_cols, 4)
            pe.wait_ge(mm_free[2], free_after(S, 2, 0))
            pe.wait_ge(mm_free[3], free_before(S, 3, 0))
            for t in range(TT):
                mm = pe.transpose(ps[3][:, t * 48:(t + 1) * 48], ngT[:, t * P:(t + 1) * P], ident[0:48, 0:48])
            mm.then_inc(mm_full[3], 1)
            for aa in range(2):
                def k_of(i, h, m, n, aa=aa):
                    return kcT[:, aa, :] if m == "c" else kT2[:, (2 if m == "w" else 0) + aa, 0:n]
                pe_attention(pe, f"N{aa}", lambda i, h, m, q: QZ2[h][:, q * P:(q + 1) * P], k_of, pv_n(aa))
            pe_attention(pe, "X", lambda i, h, m, q: QZ2[2 * h][:, q * P:(q + 1) * P],
                         lambda i, h, m, n: m2kT[:, i, :], pv_x)
            attention_over(pe, "X")
            pe_cols(pe, stages["m0"], QUAD, hh, hl, no_wait)
            S = stages["xo"]
            for s in range(2):
                pe.wait_ge(w_lo[s], S["k0"] + 1)
                for g in range(4):
                    b = 4 * s + g
                    pe.wait_ge(mm_free[b], free_before(S, b, 0))
                    for kc in range(2):
                        pe.wait_ge(ox_lo, kc + 1)
                        at = kc * 512 + g * P
                        mm = mm3(pe, ps[b][:, :], whi[s][:, at:at + P], wlo[s][:, at:at + P], oxH[:, kc, :], oxL[:, kc, :], kc == 0, kc == 1)
                    mm.then_inc(mm_full[b], 1)
            pe_cols(pe, stages["m2g"], QUAD, hh, hl, no_wait)
            pe_cols(pe, stages["wo2"], QUAD, hh, hl, hset_ready("y2"), fresh=True)
            pe_norm(pe, "g_mlp")
            for half in range(2):
                pe_cols(pe, stages[f"mu{half}"], QUAD, hh, hl, hset_ready("g_mlp"), fresh=half == 0)
                pe_cols(pe, stages[f"md{half}"], [(0,), (2,)], gh, gl, gready(f"m{half}"))
            pe_norm(pe, "g_final")
            for c in range(DC):
                pe.wait_ge(h_tmp, 8 * 6 + c + 1)
                if c >= 2:
                    pe.wait_ge(out_copied, c - 1)
                for t in range(TT):
                    mm = pe.transpose(ps[6 + c % 2][:, t * P:(t + 1) * P], htmp[c % 2][:, t * P:(t + 1) * P], ident)
                mm.then_inc(out_turned, 1)

        def act_norm_scale(act, name):
            j = NORM[name]
            act.wait_ge(stat_full, j + 1)
            act.activation(st[:, 0:4], ps[4][:, 0:4], ACT.Sqrt, bias=eps[:, 0:1], scale=1.0 / D).then_inc(sd_ready, 1)

        def act_hset(act, name, src_ready, src):
            j = HSET[name]
            for c in range(DC):
                src_ready(c)
                act.activation(hH[:, c, :], src(c), ACT.Copy).then_inc(h_hi, 1)

        def act_norm(act, name):
            act_norm_scale(act, name)
            j = NORM[name]
            act_hset(act, name, lambda c: act.wait_ge(h_tmp, 8 * j + c + 1), lambda c: htmp[c % 2][:, :])

        def act_sq(act, j, c, i=0):
            act.wait_ge(sq_used, i * 2 + (8 * j + c + 1))
            act.activation(sqb[c % 2][:, :], xT[:, i * 2 + c, :], ACT.Square).then_inc(sq_ready, 1)

        def act_ffn_up(act, n, half):
            S = stages[f"up{n}{half}"]
            g0 = G0[f"{n}{half}"]

            def body(i):
                for g in range(2):
                    act.wait_ge(mm_full[g], full(S, g, i))
                    act.wait_ge(mm_free[2 + g], free_before(S, 2 + g, i))
                    act.activation(act_t[g][:, :], ps[g][:, :], ACT.Silu).then_inc(mm_free[g], 1)
                act_split(act, S, 0, i)
                for g in range(2):
                    act.wait_ge(mm_free[2 + g], free_after(S, 2 + g, i))
                    act.activation(gH[:, i * 2 + g, :], prod[g][:, :], ACT.Copy).then_inc(g_hi, 1)
                act_split(act, S, 1, i)
            loop(act, S["its"], body)

        def act_down(act, key, j=None):
            pair = j == NORM["final"]
            S = stages[key]

            def body(i):
                for s in range(2):
                    if j is not None:
                        act.wait_ge(mm_free[2 * s], free_after(S, 2 * s, i))
                        if pair:
                            for m in range(2):
                                act.wait_ge(sq_used, i * 4 + (8 * j + 2 * s + m + 1))
                                gain = {"scale": vec[:, bass.ds(i * 2 + (VEC_COLS["final_norm"][0] + s), 1)]} if m else {}
                                act.activation(sqb[m][:, :], xT[:, i * 2 + s, :], ACT.Square, **gain).then_inc(sq_ready, 1)
                        else:
                            act_sq(act, j, s, i)
                    act_split(act, S, s, i)
            if S["name"] == LAST:
                loop(act, S["its"] - 1, body)
                body(S["its"] - 1)
            else:
                loop(act, S["its"], body)

        def act_quad(act, name, evac, after=None):
            S = stages[name]

            def body(i):
                for b in range(4):
                    act.wait_ge(mm_full[b], full(S, b, i))
                    evac(i, b)
                    if b % 2 == 1:
                        act_split(act, S, b // 2, i)
                if after:
                    after(i)
            loop(act, S["its"], body)

        def act_tok_norm(act, name, tiles, heads, tkb):
            S = stages[name]
            t0, _ = PREP[name]
            r0 = red0[name]
            act.wait_ge(sq_used, 2 + 8 * (1 if name == "mk" else NORM["mix"] + 1))
            for t in range(tiles):
                act.wait_ge(mm_full[t], full(S, t, 0))
                if r0 + t >= 2:
                    act.wait_ge(tok_red, r0 + t - 1)
                act.activation(sqb[t % 2][:, :], ps[t][:, :], ACT.Square).then_inc(tok_sq, 1)
                act.activation(tkb[:, t, :], ps[t][:, :], ACT.Copy).then_inc(mm_free[t], 1)
            if name != "cq":
                act_split(act, S, 1, 0)
            for t in range(tiles):
                act.wait_ge(tok_red, r0 + t + 1)
                act.activation(nst[:, 1, t, 0:heads], nst[:, 0, t, 0:heads],
                               ACT.Sqrt, bias=eps[:, 0:1], scale=heads / 512.0).then_inc(tok_sd, 1)
            if name == "cq":
                act_split(act, S, 1, 0)

        def act_turned(act, name, n, dst, scale=1.0, w=T):
            _, c0 = PREP[name]
            for c in range(n):
                act.wait_ge(turn_full, c0 + c + 1)
                act.activation(dst(c), ps[4 + (c0 + c) % 4][:, 0:w], ACT.Copy, scale=scale).then_inc(turn_free, 1)

        def act_plain_toks(act, name, i, dst, tiles=TT, src=lambda t: ps[t][:, :]):
            S = stages[name]
            for t in range(tiles):
                act.wait_ge(mm_full[t], full(S, t, i))
                act.activation(dst(t), src(t), ACT.Copy).then_inc(mm_free[t], 1)
            act_split(act, S, 1, i)

        @block.scalar
        def _(act):
            act.wait_ge(pool_cst, 4)
            order = Order(act, act_step)
            for m in range(2):
                act.wait_ge(mem_in[m], 16)
                for t in range(MT):
                    order(act.activation(prod_junk[:, 0:D], memx[m][:, t, :], ACT.Square, accum_out=st[:, 64 + 2 * m + t:65 + 2 * m + t]))
                act.activation(st[:, 68 + 2 * m:70 + 2 * m], st[:, 64 + 2 * m:66 + 2 * m], ACT.Sqrt, bias=eps[:, 0:1], scale=1.0 / D).then_inc(mem_sd, 1)
            act.wait_ge(cst_in, 32)
            for c in range(DC):
                act.wait_ge(xt_ready, c + 1)
                act_sq(act, 0, c)
            for s in range(2):
                act.wait_ge(w_raw[s], 16)
                act.activation(whi[s][:, :], wraw[s][:, :], ACT.Copy).then_inc(w_hi[s], 1)
            for m in range(2):
                for c in range(DC):
                    n = 4 * m + c // 2
                    act.wait_ge(mem_turned, n + 1)
                    act.activation(mH[m][:, c, :], ps[n % 4][:, (c % 2) * MEM:(c % 2 + 1) * MEM], ACT.Copy,
                                   scale=V("mem_norm" if m == 0 else "g_mem", c)).then_inc(mem_hi, 1)
            act_split(act, stages["mk"], 0, 0)
            act_tok_norm(act, "mk", MT, 4, tkM)
            act_split(act, stages["mv"], 0, 0)
            act_plain_toks(act, "mv", 0, lambda t: mv[:, t, :], MT)
            act_turned(act, "mk", 4, lambda c: mkT[:, c, :], V("c_k"), MEM)
            act_split(act, stages["m2"], 0, 0)
            S = stages["m2"]
            for t in range(MT):
                act.wait_ge(mm_full[t], full(S, t, 0))
                act.activation(m2v[:, t, :], ps[t][:, 256:512], ACT.Copy)
                act.activation(tkM[:, t, 0:256], ps[t][:, 0:256], ACT.Copy).then_inc(mm_free[t], 1)
            act_split(act, S, 1, 0)
            act_turned(act, "m2", 2, lambda c: m2kT[:, c, :], 1.0, MEM)
            act_norm(act, "ffn1")
            for half in range(2):
                act_ffn_up(act, 1, half)
                act_down(act, f"dn1{half}", NORM["mix"] if half else None)
            act.wait_ge(lam_sum, 1)
            act.activation(lamw[:, 2:4], lamw[:, 0:2], ACT.Exp).then_inc(lam_exp, 1)
            act_norm(act, "mix")
            for n, name in enumerate(("aq", "ak")):
                act_split(act, stages[name], 0, 0)
                if n:
                    act_turned(act, "aq", 4, lambda c: QT[:, c, :])
                act_tok_norm(act, name, TT, 8, tk)
            act_split(act, stages["av"], 0, 0)
            act_plain_toks(act, "av", 0, lambda t: Vt[:, t, :])
            act_turned(act, "ak", 4, lambda c: KT[:, c, :])
            act_attention(act, "A", None)
            act.wait_ge(oa_sq, 4)
            act.activation(oas[:, 1, :, :], oas[:, 0, :, :], ACT.Sqrt, bias=eps[:, 0:1], scale=1.0 / P).then_inc(oa_sd, 1)
            for n, name in enumerate(("bq", "bk")):
                act_split(act, stages[name], 0, 0)
                if n:
                    act_turned(act, "bq", 4, lambda c: QT[:, c, :], gs[:, 1:2])
                act_tok_norm(act, name, TT, 8, tk)
                if n == 0:
                    act_turned(act, "oa", 4, lambda c: oT[:, c, :], gs[:, 0:1])
            act_split(act, stages["bv"], 0, 0)
            act_plain_toks(act, "bv", 0, lambda t: Vt[:, t, :])
            act_turned(act, "bk", 4, lambda c: KT[:, c, :], V("b_k"))
            act_attention(act, "B", lambda i, g: oT[:, i + 4, :])
            act_split(act, stages["cq"], 0, 0)
            act_tok_norm(act, "cq", TT, 4, tk)
            act_turned(act, "cq", 4, lambda c: QT[:, c, :], gs[:, 2:3])
            act_attention(act, "C", lambda i, g: oT[:, i * 2 + (8 + g), :])

            def split_o(n):
                if n == 2:
                    act.wait_ge(mm_full[3], full(stages["gate0"], 3, 3))
                for c in range(4):
                    act.activation(oH[n % 2][:, c, :], oT[:, 4 * n + c, :], ACT.Copy).then_inc(o_hi, 1)
            act.wait_ge(o_free, O_RING + attn_at["C"]["O0"] + 4)
            act.wait_ge(turn_free, PREP["cq"][1] + 4)
            split_o(0)
            split_o(1)
            for n in range(3):
                S = stages[f"gate{n}"]

                def body(i, S=S, n=n):
                    for g in range(2):
                        act.wait_ge(mm_full[g], full(S, g, i))
                        act.wait_ge(mm_free[2 + g], free_before(S, 2 + g, i))
                        act.activation(sg[g][:, :], ps[g][:, :], ACT.Sigmoid,
                                       bias=vec[:, bass.ds(i * 2 + (VEC_COLS["b_gate"][0] + 8 * n + g), 1)]).then_inc(mm_free[g], 1)
                    act_split(act, S, 0, i)
                    act_split(act, S, 1, i)
                loop(act, S["its"], body)
                if n == 0:
                    split_o(2)
            j = HSET["y1"]

            def y_ready(c):
                act.wait_ge(y_done, c + 1)
            act_hset(act, "y1", y_ready, lambda c: y[:, c, :])

            def resid_evac(name, j):
                S = stages[name]

                def evac(i, b):
                    act.wait_ge(mm_free[b], free_after(S, b, i))
                    act.wait_ge(sq_used, 8 * j + 4 * i + b + 1)
                    act.activation(sqb[b % 2][:, :], xT[:, 4 * i + b, :], ACT.Square).then_inc(sq_ready, 1)
                return evac
            act_quad(act, "wo", resid_evac("wo", NORM["ffn2"]))
            act_norm(act, "ffn2")
            for half in range(2):
                act_ffn_up(act, 2, half)
                act_down(act, f"dn2{half}", NORM["final"] if half else None)
            act_norm_scale(act, "final")
            act.wait_ge(pair_ready, 1)
            act.activation(st[:, 56:60], st[:, 60:64], ACT.Sqrt, bias=eps[:, 0:1], scale=1.0 / D).then_inc(sd_ready, 1)
            act_hset(act, "g_mix", lambda c: act.wait_ge(h_tmp, 8 * NORM["final"] + c + 1), lambda c: htmp[c % 2][:, :])
            act_quad(act, "kc", lambda i, b: act.activation(kcv[:, b, :], ps[b][:, :], ACT.Copy).then_inc(mm_free[b], 1))
            act.wait_ge(spilled, 16)
            act_quad(act, "gr", lambda i, b: act.activation(gg[:, 4 * i + b, :], ps[b][:, :], ACT.Gelu_apprx_tanh).then_inc(mm_free[b], 1))
            for m in range(2):
                for hc in range(2):
                    act.wait_ge(cmp_h, 2 * m + hc + 1)
                    if m and not hc:
                        act.wait_ge(cmp_o, 1)
                    act.activation(hid[:, hc, :], ps[4 + hc][:, 0:4 * NCMP], ACT.Gelu_apprx_tanh).then_inc(cmp_hid, 1)
                act.wait_ge(cmp_o, m + 1)
                dst = kct[:, :, :] if m == 0 else vcp[0:NCMP, :, :]
                act.activation(dst, ps[6 + m][0:NCMP, 0:256].rearrange("p (g d) -> p g d", g=4), ACT.Copy).then_inc(cmp_copied, 1)
            act.wait_ge(cmp_turn, 1)
            act.activation(kcT[:, :, 0:NCMP], ps[6][:, 256:256 + 2 * NC32].rearrange("p (a n) -> p a n", a=2)[:, :, 0:NCMP], ACT.Copy)
            act.wait_ge(cmp_copied, 2)
            act.activation(lamw[:, 6:7], lamw[:, 4:5], ACT.Copy).then_inc(vc_done, 1)

            def x_evac(i, b):
                c = 4 * i + b
                if c >= 2:
                    act.wait_ge(xc_ready, c - 1)
                act.activation(xp[c % 2][:, 3:T + 3], ps[b][:, :], ACT.Copy).then_inc(mm_free[b], 1)
            act.wait_ge(xp_zero, 2)
            act_quad(act, "xr", x_evac)
            act.wait_ge(sp_in, 1)
            act.activation(sp8[:, 1, :], sp8[:, 0, :], ACT.Exp, scale=-1.0).then_inc(sp_exp, 1)
            for c in range(DC):
                for m, (t, n) in enumerate(((rg, "b_rg_a"), (gi, "b_rg_i"))):
                    act.wait_ge(rg_full, 2 * c + m + 1)
                    act.activation(t[:, c, :], ps[4 + 2 * (c % 2) + m][:, :], ACT.Sigmoid, bias=V(n, c)).then_inc(rg_sig, 1)
            act.wait_ge(sp_ready, 1)
            act.wait_ge(rg_sig, 16)
            for c in range(DC):
                act.activation(av[:, c, :], rg[:, c, :], ACT.Exp, scale=sp8[:, 6, c:c + 1]).then_inc(rg_a, 1)
                act.wait_ge(rg_a, c + 1)
                act.activation(rg[:, c, :], rg[:, c, :], ACT.Tanh, scale=sp8[:, 7, c:c + 1]).then_inc(rg_t, 1)

            def gate_evac(used):
                def evac(i, b):
                    n = 4 * i + b
                    if used + n >= 2:
                        act.wait_ge(merged, used + n - 1)
                    act.activation(sgm[n % 2][:, :], ps[b][:, :], ACT.Sigmoid).then_inc(mm_free[b], 1)
                return evac
            act_quad(act, "m1", gate_evac(0))
            for c in range(DC):
                act.wait_ge(rg_m2, c + 1)
                act.activation(rg[:, c, :], rg[:, c, :], ACT.Sqrt).then_inc(rg_mult, 1)
            act.wait_ge(y1_done, DC)
            for n in range(2):
                act_split(act, stages["q"], 0, n)
                if n:
                    act_turned(act, "q0", 4, lambda c: q2[:, c, :], 0.125)
                act_plain_toks(act, "q", n, lambda t: tk2[:, t, :].rearrange("p (j g d) -> p g j d", g=2, j=4),
                               src=lambda t: ps[t][:, :].rearrange("p (g j d) -> p g j d", g=2, j=4))
            for n, name in enumerate(("ksv", "kwv")):
                S = stages[name]
                act_split(act, S, 0, 0)
                if n == 0:
                    act_turned(act, "q1", 4, lambda c: q2[:, 4 + c, :], 0.125)
                for t in range(TT):
                    act.wait_ge(mm_full[t], full(S, t, 0))
                    act.activation(tk2[:, t, 256 * n:256 * n + 256], ps[t][:, 0:256], ACT.Copy)
                    act.activation(v2[:, t, 256 * n:256 * n + 256], ps[t][:, 256:512], ACT.Copy).then_inc(mm_free[t], 1)
                act_split(act, S, 1, 0)
            S = stages["qx"]
            for g in range(2):
                act.wait_ge(mm_full[g], full(S, g, 0))
                act.activation(qx[:, g, :], ps[g][:, :], ACT.Copy, scale=0.125).then_inc(mm_free[g], 1)
            act_split(act, S, 0, 0)
            act.wait_ge(mm_full[2], full(S, 2, 0))
            act.activation(ngT[:, :], ps[2][0:48, :], ACT.Copy).then_inc(mm_free[2], 1)
            act_turned(act, "kk", 4, lambda c: kT2[:, c, :])
            act.wait_ge(mm_full[3], full(S, 3, 0))
            act.activation(ng[:, :, :], ps[3][:, 0:192].rearrange("p (q n) -> p q n", q=TT), ACT.Sigmoid).then_inc(mm_free[3], 1)
            act_split(act, S, 1, 0)
            for aa in range(2):
                act_attention(act, f"N{aa}", lambda i, g, aa=aa: yn[:, 4 * aa + 2 * g + i, :])
            act_attention(act, "X", lambda i, g: ox[:, i, :])
            act.wait_ge(o_free, O_RING + attn_at["X"]["O0"] + 2)
            for c in range(2):
                act.activation(oxH[:, c, :], ox[:, c, :], ACT.Copy).then_inc(ox_hi, 1)
            act_quad(act, "m0", gate_evac(8))
            S = stages["xo"]
            for s in range(2):
                for g in range(4):
                    b = 4 * s + g
                    act.wait_ge(mm_full[b], full(S, b, 0))
                    act.activation(yx[:, b, :], ps[b][:, :], ACT.Copy).then_inc(mm_free[b], 1)
                act_split(act, S, s, 0)
            act_quad(act, "m2g", gate_evac(16))
            act_hset(act, "y2", lambda c: act.wait_ge(y2_done, c + 1), lambda c: yacc[:, c, :])
            act.wait_ge(spill_back, 16)
            act_quad(act, "wo2", resid_evac("wo2", NORM["g_mlp"]))
            act_norm(act, "g_mlp")
            for half in range(2):
                S = stages[f"mu{half}"]

                def body(i, S=S, half=half):
                    g0 = 16 * half
                    for b in range(4):
                        act.wait_ge(mm_full[b], full(S, b, i))
                        act.wait_ge(g_prod, i * 4 + (g0 + b + 1))
                        act.activation(act_t[b % 2][:, :], ps[b][:, :], ACT.Relu).then_inc(mm_free[b], 1)
                        if b:
                            act.wait_ge(g_prod, i * 4 + (g0 + b + 2))
                            act.activation(gH[:, i * 4 + (b - 1), :], prod[(b - 1) % 2][:, :], ACT.Copy).then_inc(g_hi, 1)
                        if b == 1:
                            act_split(act, S, 0, i)
                    act.wait_ge(g_prod, i * 4 + (g0 + 6))
                    act.activation(gH[:, i * 4 + 3, :], prod[1][:, :], ACT.Copy).then_inc(g_hi, 1)
                    act_split(act, S, 1, i)
                loop(act, S["its"], body)
                act_down(act, f"md{half}", NORM["g_final"] if half else None)
            act_norm_scale(act, "g_final")
            for c in range(DC):
                act.wait_ge(out_turned, c + 1)
                act.activation(xin[:, :, c * P:(c + 1) * P], ps[6 + c % 2][:, :].rearrange("p (q d) -> p q d", q=TT), ACT.Copy).then_inc(out_copied, 1)

        def dve_norm_scale(dve, order, name):
            j = NORM[name]
            dve.wait_ge(sd_ready, j + 1)
            order(dve.reciprocal(st[:, 4:8], st[:, 0:4]))
            dve.tensor_tensor(diag[:, :, :], ident.unsqueeze(1).broadcast_to([P, TT, P]),
                              st[:, 4:8].unsqueeze(2).broadcast_to([P, TT, P]), ALU.mult).then_inc(diag_ready, 1)
            dve.wait_ge(rr_full, j + 1)

        def dve_lo(dve, j, c, src):
            dve.wait_ge(h_hi, 8 * j + c + 1)
            dve.tensor_tensor(hL[:, c, :], src, f32(hH[:, c, :]), ALU.subtract).then_inc(h_lo, 1)

        def dve_norm(dve, order, name):
            dve_norm_scale(dve, order, name)
            dve_norm_chunks(dve, name)

        def dve_norm_chunks(dve, name):
            j = HSET[name]
            for c in range(DC + 1):
                if c < DC:
                    if c >= 2:
                        dve.wait_ge(h_lo, 8 * j + c - 1)
                    dve.scalar_tensor_tensor(htmp[c % 2][:, :], xT[:, c, :], V(GAIN[name], c), ps[5][:, :],
                                             ALU.mult, ALU.mult).then_inc(h_tmp, 1)
                if c:
                    dve_lo(dve, j, c - 1, htmp[(c - 1) % 2][:, :])

        def dve_ffn_up(dve, n, half):
            S = stages[f"up{n}{half}"]
            g0 = G0[f"{n}{half}"]

            def body(i):
                dve_split(dve, S, 0, i)
                for g in range(2):
                    dve.wait_ge(mm_full[2 + g], full(S, 2 + g, i))
                    dve.wait_ge(mm_free[g], free_after(S, g, i))
                    dve.tensor_tensor(prod[g][:, :], act_t[g][:, :], ps[2 + g][:, :], ALU.mult).then_inc(mm_free[2 + g], 1)
                for g in range(2):
                    dve.wait_ge(g_hi, i * 2 + (g0 + g + 1))
                    dve.tensor_tensor(gL[:, i * 2 + g, :], prod[g][:, :], f32(gH[:, i * 2 + g, :]), ALU.subtract).then_inc(g_lo, 1)
                dve_split(dve, S, 1, i)
            loop(dve, S["its"], body)

        def dve_down(dve, key, scale):
            S = stages[key]

            def body(i):
                for s in range(2):
                    dve.wait_ge(mm_full[2 * s], full(S, 2 * s, i))
                    x_ = xT[:, i * 2 + s, :]
                    dve.scalar_tensor_tensor(x_, ps[2 * s][:, :], scale, x_, ALU.mult, ALU.add).then_inc(mm_free[2 * s], 1)
                    dve_split(dve, S, s, i)
            if S["name"] == LAST:
                loop(dve, S["its"] - 1, body)
                body(S["its"] - 1)
            else:
                loop(dve, S["its"], body)

        def dve_quad(dve, name, work=None):
            S = stages[name]

            def body(i):
                for b in range(4):
                    if work:
                        work(i, b)
                    if b % 2 == 1:
                        dve_split(dve, S, b // 2, i)
            loop(dve, S["its"], body)

        def dve_tok_norm(dve, order, name, tiles, heads, tkb, rope=None):
            S = stages[name]
            t0, _ = PREP[name]
            r0 = red0[name]
            d = 512 // heads
            for t in range(tiles):
                dve.wait_ge(tok_sq, r0 + t + 1)
                dve.tensor_reduce(nst[:, 0, t, 0:heads], sqb[t % 2][:, :].rearrange("p (h d) -> p h d", h=heads), AX.X, ALU.add).then_inc(tok_red, 1)
            if name != "cq":
                dve_split(dve, S, 1, 0)
            for t in range(tiles):
                dve.wait_ge(tok_sd, r0 + t + 1)
                order(dve.reciprocal(nst[:, 2, t, 0:heads], nst[:, 1, t, 0:heads]))
                dve.wait_ge(mm_free[t], free_after(S, t, 0))
                v = tkb[:, t, :].rearrange("p (h d) -> p h d", h=heads)
                r = nst[:, 2, t, 0:heads].unsqueeze(2).broadcast_to([P, heads, d])
                if rope is None:
                    dve.tensor_tensor(v, v, r, ALU.mult).then_inc(tok_ready, 1)
                else:
                    order(dve.tensor_tensor(v, v, r, ALU.mult))
                    c_ = rtab[:, rope, t, :].unsqueeze(1).broadcast_to([P, heads, HD])
                    s_ = rtab[:, rope + 1, t, :].unsqueeze(1).broadcast_to([P, heads, HD])
                    t1 = rt[0][:, :].rearrange("p (h d) -> p h d", h=heads)
                    t2 = rt[1][:, :].rearrange("p (h d) -> p h d", h=heads)
                    dve.tensor_tensor(t1, v, c_, ALU.mult)
                    dve.tensor_tensor(t2[:, :, 0:32], v[:, :, 32:64], s_[:, :, 0:32], ALU.mult)
                    order(dve.tensor_tensor(t2[:, :, 32:64], v[:, :, 0:32], s_[:, :, 32:64], ALU.mult))
                    dve.tensor_tensor(v, t1, t2, ALU.add).then_inc(tok_ready, 1)
            if name == "cq":
                dve_split(dve, S, 1, 0)

        def dve_tok_rope(dve, order, name, stage_name, i):
            S = stages[stage_name]
            for t in range(TT):
                dve.wait_ge(mm_free[t], free_after(S, t, i))
                v = tk2[:, t, :].rearrange("p (h d) -> p h d", h=8)
                x1, x2 = v[:, :, 0:8], v[:, :, 8:16]
                c_ = C("cosN")[:, 8 * t:8 * t + 8].unsqueeze(1).broadcast_to([P, 8, 8])
                s_ = C("sinN")[:, 8 * t:8 * t + 8].unsqueeze(1).broadcast_to([P, 8, 8])
                for n, (x_, f_) in enumerate(((x1, c_), (x2, s_), (x2, c_), (x1, s_))):
                    ins = dve.tensor_tensor(rn[n][:, :, :], x_, f_, ALU.mult)
                order(ins)
                dve.tensor_tensor(x1, rn[0][:, :, :], rn[1][:, :, :], ALU.subtract)
                dve.tensor_tensor(x2, rn[2][:, :, :], rn[3][:, :, :], ALU.add).then_inc(tok_ready, 1)
                if t < TT - 1:
                    dve.wait_ge(tok_ready, PREP[name][0] + t + 1)
            dve_split(dve, S, 1, i)

        @block.vector
        def _(dve):
            order = Order(dve, dve_step)
            for b in range(8):
                dve.memset(st[:, 80 + b:81 + b], 0.0).then_inc(mm_free[b], 1)
            dve.memset(st[:, 88:89], 0.0).then_inc(t_free, T_RING)
            dve.memset(st[:, 89:90], 0.0).then_inc(pv_done, PV_RING)
            dve.memset(st[:, 90:91], 0.0).then_inc(o_free, O_RING)
            dve.memset(st[:, 91:92], 0.0).then_inc(g_prod, 2)
            dve.wait_ge(cst_in, 32)
            dve.tensor_scalar(gs[:, 0:1], V("a_sub"), 1.0 - LAMBDA_INIT, None, ALU.mult)
            dve.tensor_scalar(gs[:, 1:2], V("b_q"), HD ** -0.5, None, ALU.mult)
            dve.tensor_scalar(gs[:, 2:3], V("c_q"), P ** -0.5, None, ALU.mult)
            dve.tensor_tensor(V("g_mix", 0, 8), V("g_mix", 0, 8), V("final_norm", 0, 8), ALU.mult)
            order(dve.tensor_tensor(V("lam", 0, 64), V("lam", 0, 64), V("lam", 64, 64), ALU.mult))
            order(dve.tensor_tensor(V("lam", 128, 64), V("lam", 128, 64), V("lam", 192, 64), ALU.mult))
            dve.tensor_reduce(lamw[:, 0:1], V("lam", 0, 64), AX.X, ALU.add)
            dve.tensor_reduce(lamw[:, 1:2], V("lam", 128, 64), AX.X, ALU.add).then_inc(lam_sum, 1)
            for m in range(2):
                dve.wait_ge(mem_sd, m + 1)
                order(dve.reciprocal(st[:, 72 + 2 * m:74 + 2 * m], st[:, 68 + 2 * m:70 + 2 * m]))
                for t in range(MT):
                    ins = dve.tensor_scalar(memx[m][:, t, :], memx[m][:, t, :], st[:, 72 + 2 * m + t:73 + 2 * m + t], None, ALU.mult)
                ins.then_inc(mem_norm_ready, 1)
            for c in range(DC):
                dve.wait_ge(x_turned, c + 1)
                dve.tensor_copy(xT[:, c, :], ps[6 + c % 2][:, :]).then_inc(xt_ready, 1)
            for s in range(2):
                dve.wait_ge(w_hi[s], 1)
                dve.tensor_tensor(wlo[s][:, :], wraw[s][:, :], f32(whi[s][:, :]), ALU.subtract).then_inc(w_lo[s], 1)
            for m in range(2):
                for c in range(DC):
                    n = 4 * m + c // 2
                    dve.wait_ge(mem_hi, 2 * n + 2)
                    dve.scalar_tensor_tensor(mL[m][:, c, :], ps[n % 4][:, (c % 2) * MEM:(c % 2 + 1) * MEM],
                                             V("mem_norm" if m == 0 else "g_mem", c), f32(mH[m][:, c, :]),
                                             ALU.mult, ALU.subtract).then_inc(mem_lo, 1)
            dve_split(dve, stages["mk"], 0, 0)
            dve_tok_norm(dve, order, "mk", MT, 4, tkM)
            for n in ("mv", "m2"):
                for s in range(2):
                    dve_split(dve, stages[n], s, 0)
            dve_norm(dve, order, "ffn1")
            for half in range(2):
                dve_ffn_up(dve, 1, half)
                dve_down(dve, f"dn1{half}", 0.5)
            dve.wait_ge(lam_exp, 1)
            order(dve.tensor_tensor(lamw[:, 4:5], lamw[:, 3:4], lamw[:, 2:3], ALU.subtract))
            dve.tensor_scalar(gs[:, 3:4], lamw[:, 4:5], -LAMBDA_INIT, None, ALU.add)
            dve_norm(dve, order, "mix")
            cos_, sin_ = (C(n).rearrange("p (q d) -> p q d", q=TT) for n in ("cosA", "sinA"))
            for r, (n, scale) in enumerate((("a_qg", HD ** -0.5), ("a_kg", 1.0))):
                g_ = lambda a_, b_: V(n, a_, b_).unsqueeze(1).broadcast_to([P, TT, b_])
                if scale != 1.0:
                    order(dve.tensor_scalar(V(n, 0, 64), V(n, 0, 64), scale, None, ALU.mult))
                dve.tensor_tensor(rtab[:, 2 * r, :, :], cos_, g_(0, 64), ALU.mult)
                dve.tensor_tensor(rtab[:, 2 * r + 1, :, 0:32], sin_[:, :, 0:32], g_(32, 32), ALU.mult)
                order(dve.tensor_tensor(rtab[:, 2 * r + 1, :, 32:64], sin_[:, :, 32:64], g_(0, 32), ALU.mult))
            for r, name in enumerate(("aq", "ak")):
                dve_split(dve, stages[name], 0, 0)
                dve_tok_norm(dve, order, name, TT, 8, tk, rope=2 * r)
            for s in range(2):
                dve_split(dve, stages["av"], s, 0)

            def after_turns(name, v=None):
                dve.wait_ge(turn_free, PREP[name][1] + 4)
                if v:
                    dve.wait_ge(mm_free[3], free_after(stages[v], 3, 0))

            def stage_a(i):
                for h in range(2):
                    for m in range(2):
                        r = slice(HD * m, HD * m + HD)
                        ins = dve.tensor_copy(QZ[2 * h + m][r, :], QT[r, i * 2 + h, :])
                ins.then_inc(staged, 1)
            after_turns("ak", "av")
            dve.wait_ge(qz_zero, 4)
            mask1 = lambda t, n: C("mask_chunk")[:, T - n:T]
            dve_attention(dve, order, "A", stage_a, mask1)
            dve.wait_ge(oa_sd, 1)
            order(dve.reciprocal(oas[:, 2, :, :], oas[:, 1, :, :]))
            dve.wait_ge(o_free, O_RING + attn_at["B"]["O0"])
            for h in range(4):
                v = oT[:, h, :].rearrange("p (q d) -> p q d", q=TT)
                dve.tensor_tensor(v, v, oas[:, 2, h, :].unsqueeze(2).broadcast_to([P, TT, P]), ALU.mult).then_inc(oa_ready, 1)
            for name in ("bq", "bk"):
                dve_split(dve, stages[name], 0, 0)
                dve_tok_norm(dve, order, name, TT, 8, tk)
            for s in range(2):
                dve_split(dve, stages["bv"], s, 0)
            after_turns("bk", "bv")

            def stage_b(i):
                dve.wait_ge(pv_done, M_(attn_at["B"], i, 0) + PV_RING)
                for h in range(2):
                    r = slice(HD * h, HD * h + HD)
                    dve.tensor_copy(QZ[h][r, :], QT[r, i, :])
                dve.tensor_copy(vst[:, :, :], Vt[:, :, bass.ds(i * P, P)]).then_inc(staged, 1)
            dve_attention(dve, order, "B", stage_b, lambda t, n: bias2[t % 2][:, T - n:T])
            dve_split(dve, stages["cq"], 0, 0)
            dve_tok_norm(dve, order, "cq", TT, 4, tk)
            after_turns("cq")

            def stage_c(i):
                dve.wait_ge(pv_done, M_(attn_at["C"], i, 0) + PV_RING)
                for h in range(2):
                    dve.tensor_copy(QZ[h][:, :], QT[:, i * 2 + h, :])
                    ins = dve.tensor_copy(vst[:, 2 * h:2 * h + 2, :], mv[:, :, bass.ds((i * 2 + h) * P, P)])
                ins.then_inc(staged, 1)
            dve_attention(dve, order, "C", stage_c, lambda t, n: C("mask_chunk")[:, 0:n])

            def split_o(n):
                for c in range(4):
                    dve.wait_ge(o_hi, 4 * n + c + 1)
                    dve.tensor_tensor(oL[n % 2][:, c, :], oT[:, 4 * n + c, :], f32(oH[n % 2][:, c, :]), ALU.subtract).then_inc(o_lo, 1)
            split_o(0)
            split_o(1)
            for n in range(3):
                S = stages[f"gate{n}"]

                def body(i, S=S, n=n):
                    dve_split(dve, S, 0, i)
                    for g in range(2):
                        dve.wait_ge(mm_full[2 + g], full(S, 2 + g, i))
                        dve.wait_ge(mm_free[g], free_after(S, g, i))
                        yc = y[:, i * 2 + g, :]
                        dst = yc if n == 0 else gt[g][:, :]
                        dve.tensor_tensor(dst, sg[g][:, :], ps[2 + g][:, :], ALU.mult).then_inc(mm_free[2 + g], 1)
                        if n:
                            dve.wait_ge(mm_free[2 + g], free_after(S, 2 + g, i))
                            ins = dve.tensor_tensor(yc, yc, gt[g][:, :], ALU.add)
                            if n == 2:
                                ins.then_inc(y_done, 1)
                    dve_split(dve, S, 1, i)
                loop(dve, S["its"], body)
                if n == 0:
                    split_o(2)
            for c in range(DC):
                dve_lo(dve, HSET["y1"], c, y[:, c, :])

            def resid(name):
                S = stages[name]

                def work(i, b):
                    dve.wait_ge(mm_full[b], full(S, b, i))
                    x_ = xT[:, 4 * i + b, :]
                    dve.tensor_tensor(x_, ps[b][:, :], x_, ALU.add).then_inc(mm_free[b], 1)
                return work
            dve_quad(dve, "wo", resid("wo"))
            dve_norm(dve, order, "ffn2")
            for half in range(2):
                dve_ffn_up(dve, 2, half)
                dve_down(dve, f"dn2{half}", 0.5)
            j = NORM["final"]
            dve.wait_ge(sd_ready, j + 1)
            order(dve.reciprocal(st[:, 4:8], st[:, 0:4]))
            dve.wait_ge(stat_full, j + 2)
            order(dve.tensor_tensor(st[:, 60:64], ps[7][:, 0:4], st[:, 4:8], ALU.mult))
            dve.tensor_tensor(st[:, 60:64], st[:, 60:64], st[:, 4:8], ALU.mult).then_inc(pair_ready, 1)
            dve.wait_ge(sd_ready, j + 2)
            order(dve.reciprocal(st[:, 76:80], st[:, 56:60]))
            order(dve.tensor_tensor(st[:, 76:80], st[:, 76:80], st[:, 4:8], ALU.mult))
            for m, at in enumerate((76, 4)):
                if m:
                    dve.wait_ge(rr_full, j + 1)
                dve.tensor_tensor(diag[:, :, :], ident.unsqueeze(1).broadcast_to([P, TT, P]),
                                  st[:, at:at + 4].unsqueeze(2).broadcast_to([P, TT, P]), ALU.mult).then_inc(diag_ready, 1)
            dve_norm_chunks(dve, "g_mix")
            dve.wait_ge(rr_full, j + 2)
            dve.wait_ge(h_lo, 8 * (HSET["g_mix"] + 1))
            for c in range(DC):
                dve.scalar_tensor_tensor(xT[:, c, :], xT[:, c, :], V("final_norm", c), ps[6][:, :], ALU.mult, ALU.mult).then_inc(h_tmp, 1)
            for s in range(2):
                dve_split(dve, stages["kc"], s, 0)
            def blocks(m):
                dve.wait_ge(z_in[m], 16 * 8)
                for k in range(16):
                    if m and not k:
                        dve.wait_ge(cmp_h, 2)
                    dve.tensor_scalar(RB[:, k, :, :], Z[m][:, :, 2 * k:2 * k + 16 * (NCMP - 1) + 1:16],
                                      V("pos_k" if m == 0 else "pos_v", k), None, ALU.add).then_inc(cmp_rb, 1)
            dve_quad(dve, "gr", lambda i, b: blocks(0) if (i, b) == (1, 0) else None)
            blocks(1)
            dve.wait_ge(cmp_copied, 1)
            x1, x2 = kct[:, :, 0:8], kct[:, :, 8:16]
            c_ = C("cosC")[0:NCMP, :].unsqueeze(1).broadcast_to([NCMP, 4, 8])
            s_ = C("sinC")[0:NCMP, :].unsqueeze(1).broadcast_to([NCMP, 4, 8])
            r_ = [crn[:, n, :, :] for n in range(4)]
            for n, (x_, f_) in enumerate(((x1, c_), (x2, s_), (x2, c_), (x1, s_))):
                ins = dve.tensor_tensor(r_[n], x_, f_, ALU.mult)
            order(ins)
            dve.tensor_tensor(x1, r_[0], r_[1], ALU.subtract)
            dve.tensor_tensor(x2, r_[2], r_[3], ALU.add).then_inc(cmp_rope, 1)
            dve.wait_ge(vc_done, 1)
            dve.memset(xp[0][:, 0:3], 0.0).then_inc(xp_zero, 1)
            dve.memset(xp[1][:, 0:3], 0.0).then_inc(xp_zero, 1)
            L = lambda n: sp8[:, n, :]
            order(dve.tensor_scalar(L(5), V("rg_lambda", 0, 8), -1.0, None, ALU.mult))
            dve.tensor_tensor(L(0), L(5), V("rg_lambda", 0, 8), ALU.max).then_inc(sp_in, 1)

            def conv(i, b):
                c = 4 * i + b
                dve.wait_ge(mm_free[b], free_after(stages["xr"], b, i))
                w = lambda k: V("conv_w", 8 * k + c)
                order(dve.tensor_scalar(xc[:, c, :], xp[c % 2][:, 0:T], w(0), V("conv_b", c), ALU.mult, ALU.add))
                for k in range(1, 4):
                    ins = dve.scalar_tensor_tensor(xc[:, c, :], xp[c % 2][:, k:T + k], w(k), xc[:, c, :], ALU.mult, ALU.add)
                    if k < 3:
                        order(ins)
                ins.then_inc(xc_ready, 1)
            dve_quad(dve, "xr", conv)
            dve.wait_ge(sp_exp, 1)
            order(dve.tensor_scalar(L(2), L(1), 2.0, None, ALU.add))
            order(dve.reciprocal(L(3), L(2)))
            order(dve.tensor_tensor(L(2), L(1), L(3), ALU.mult))
            order(dve.tensor_tensor(L(3), L(2), L(2), ALU.mult))
            order(dve.tensor_scalar(L(4), L(3), 1.0 / 17, 1.0 / 15, ALU.mult, ALU.add))
            for k in (13, 11, 9, 7, 5, 3, 1):
                order(dve.tensor_tensor(L(4), L(4), L(3), ALU.mult))
                order(dve.tensor_scalar(L(4), L(4), 1.0 / k, None, ALU.add))
            order(dve.tensor_tensor(L(4), L(4), L(2), ALU.mult))
            order(dve.tensor_scalar(L(4), L(4), 2.0, None, ALU.mult))
            order(dve.tensor_scalar(L(5), L(5), 0.0, None, ALU.max))
            order(dve.tensor_tensor(L(4), L(4), L(5), ALU.add))
            dve.tensor_scalar(L(6), L(4), -8.0, None, ALU.mult)
            dve.tensor_scalar(L(7), L(4), 8.0, None, ALU.mult).then_inc(sp_ready, 1)
            for c in range(DC):
                dve.wait_ge(rg_sig, 2 * c + 2)
                order(dve.tensor_tensor(gi[:, c, :], gi[:, c, :], xc[:, c, :], ALU.mult))
            for c in range(DC):
                dve.wait_ge(rg_t, c + 1)
                order(dve.tensor_tensor(rt2[c % 2][:, :], av[:, c, :], av[:, c, :], ALU.mult))
                dve.scalar_tensor_tensor(rg[:, c, :], rt2[c % 2][:, :], 1.0, rg[:, c, :], ALU.add, ALU.mult).then_inc(rg_m2, 1)
            S1 = stages["m1"]

            def merge1(i, b):
                c = 4 * i + b
                dve.wait_ge(mm_free[b], free_after(S1, b, i))
                dve.tensor_tensor(gg[:, c, :], gg[:, c, :], sgm[c % 2][:, :], ALU.mult).then_inc(merged, 1)
            dve_quad(dve, "m1", merge1)
            for c in range(DC):
                dve.wait_ge(rg_mult, c + 1)
                order(dve.tensor_tensor(gi[:, c, :], gi[:, c, :], rg[:, c, :], ALU.mult))
                order(dve.tensor_tensor_scan(rg[:, c, :], av[:, c, :], gi[:, c, :], 0.0, ALU.mult, ALU.add))
                dve.tensor_tensor(yacc[:, c, :], gg[:, c, :], rg[:, c, :], ALU.mult).then_inc(y1_done, 1)
            for n in range(2):
                dve_split(dve, stages["q"], 0, n)
                dve_tok_rope(dve, order, f"q{n}", "q", n)
            for s in range(2):
                dve_split(dve, stages["ksv"], s, 0)
            dve_split(dve, stages["kwv"], 0, 0)
            dve_tok_rope(dve, order, "kk", "kwv", 0)
            dve_split(dve, stages["qx"], 0, 0)
            dve.wait_ge(mm_free[3], free_after(stages["qx"], 3, 0))
            order(dve.tensor_tensor(ng[:, :, 0:48:3], ng[:, :, 0:48:3], C("valid").unsqueeze(2).broadcast_to([P, TT, 16]), ALU.mult))
            dve_split(dve, stages["qx"], 1, 0)
            dve.wait_ge(turn_free, PREP["kk"][1] + 4)
            dve.wait_ge(qz_zero, 10)
            for aa in range(2):
                def stage_n(i, aa=aa):
                    for h in range(4):
                        r = slice(HD * (h // 2), HD * (h // 2) + HD)
                        ins = dve.tensor_copy(QZ2[h][r, :], q2[r, 4 * aa + 2 * i + h % 2, :])
                    ins.then_inc(staged, 1)

                def gate_of(i, h, m, qt, aa=aa):
                    col = 3 * ((2 * aa + h // 2) * 4 + 2 * i + h % 2) + "csw".index(m)
                    return ng[:, :, col] if qt is None else ng[:, qt, col:col + 1]
                dve_attention(dve, order, f"N{aa}", stage_n, lambda t, n: C("mask_causal")[:, T - n:T], gate_of)

            def stage_x(i):
                for h in range(2):
                    r = slice(HD * h, HD * h + HD)
                    ins = dve.tensor_copy(QZ2[2 * h][r, :], qx[r, i, :])
                ins.then_inc(staged, 1)
            dve_attention(dve, order, "X", stage_x, lambda t, n: C("mask_chunk")[:, 0:n])
            for c in range(2):
                dve.wait_ge(ox_hi, c + 1)
                dve.tensor_tensor(oxL[:, c, :], ox[:, c, :], f32(oxH[:, c, :]), ALU.subtract).then_inc(ox_lo, 1)

            def merge(S, used, src, last):
                def work(i, b):
                    c = 4 * i + b
                    dve.wait_ge(mm_free[b], free_after(S, b, i))
                    dve.tensor_tensor(src[:, c, :], src[:, c, :], sgm[c % 2][:, :], ALU.mult).then_inc(merged, 1)
                    dve.wait_ge(merged, used + c + 1)
                    ins = dve.tensor_tensor(yacc[:, c, :], yacc[:, c, :], src[:, c, :], ALU.add)
                    if last:
                        ins.then_inc(y2_done, 1)
                return work
            dve_quad(dve, "m0", merge(stages["m0"], 8, yn, False))
            for s in range(2):
                dve_split(dve, stages["xo"], s, 0)
            dve_quad(dve, "m2g", merge(stages["m2g"], 16, yx, True))
            for c in range(DC):
                dve_lo(dve, HSET["y2"], c, yacc[:, c, :])
            dve.wait_ge(spill_back, 16)
            dve_quad(dve, "wo2", resid("wo2"))
            dve_norm(dve, order, "g_mlp")
            for half in range(2):
                S = stages[f"mu{half}"]

                def body(i, S=S, half=half):
                    g0 = 16 * half
                    k0 = G0[f"m{half}"]

                    def lo(c):
                        dve.wait_ge(g_hi, i * 4 + (k0 + c + 1))
                        dve.tensor_tensor(gL[:, i * 4 + c, :], prod[c % 2][:, :], f32(gH[:, i * 4 + c, :]), ALU.subtract).then_inc(g_lo, 1)
                    for b in range(4):
                        dve.wait_ge(mm_free[b], free_after(S, b, i))
                        dve.wait_ge(g_lo, i * 4 + (k0 + b - 1))
                        dve.tensor_tensor(prod[b % 2][:, :], act_t[b % 2][:, :], act_t[b % 2][:, :], ALU.mult).then_inc(g_prod, 1)
                        if b:
                            lo(b - 1)
                        if b == 1:
                            dve_split(dve, S, 0, i)
                    lo(3)
                    dve_split(dve, S, 1, i)
                loop(dve, S["its"], body)
                dve_down(dve, f"md{half}", 1.0)
            dve_norm_scale(dve, order, "g_final")
            for c in range(DC):
                if c >= 2:
                    dve.wait_ge(out_turned, c - 1)
                dve.scalar_tensor_tensor(htmp[c % 2][:, :], xT[:, c, :], V("g_final", c), ps[5][:, :], ALU.mult, ALU.mult).then_inc(h_tmp, 1)


_INS = ("x", "mem", "ffn1_wg", "ffn1_wu", "ffn1_wd", "w_in", "w_mem_kv", "w_gate", "w_branch", "w_out",
        "ffn2_wg", "ffn2_wu", "ffn2_wd", "mem_2", "w_in_2", "w_cmp_k1_2", "w_cmp_k2_2", "w_cmp_v1_2", "w_cmp_v2_2",
        "w_rg_a_2", "w_rg_i_2", "w_mem_kv_2", "w_xo_2", "w_o_2", "w_up_2", "w_down_2")


def lay_out(inputs):
    arrays = {n: np.ascontiguousarray(inputs[n]) for n in _INS}
    vec = np.zeros((P, NVEC), np.float32)

    def put(name, a):
        at, n = VEC_COLS[name]
        vec[:, at:at + n] = a

    def by_chunk(a):
        return np.moveaxis(np.asarray(a).reshape(-1, P), 1, 0)

    g = {n: np.asarray(v) for n, v in inputs.items()}
    for name, src in (("ffn1_norm", "ffn1_norm"), ("mix_norm", "mix_norm"), ("mem_norm", "mem_norm"),
                      ("ffn2_norm", "ffn2_norm"), ("final_norm", "final_norm"), ("g_mix", "g_mix_2"),
                      ("g_mem", "g_mem_2"), ("g_mlp", "g_mlp_2"), ("g_final", "g_final_2"), ("a_sub", "a_sub_norm"),
                      ("c_q", "c_q_norm"), ("c_k", "c_k_norm"), ("b_gate", "b_gate"), ("conv_w", "conv_w_2"),
                      ("conv_b", "conv_b_2"), ("b_rg_a", "b_rg_a_2"), ("b_rg_i", "b_rg_i_2"), ("rg_lambda", "rg_lambda_2"),
                      ("pos_k", "cmp_pos_k_2"), ("pos_v", "cmp_pos_v_2")):
        put(name, by_chunk(g[src]))
    for name, src in (("b_q", "b_q_norm"), ("b_k", "b_k_norm")):
        put(name, np.concatenate([g[src][0], g[src][0]])[:, None])
    put("lam", np.broadcast_to(g["a_lambda"].reshape(1, 256), (P, 256)))
    put("a_qg", np.broadcast_to(g["a_q_norm"].reshape(1, HD), (P, HD)))
    put("a_kg", np.broadcast_to(g["a_k_norm"].reshape(1, HD), (P, HD)))
    arrays["vec"] = vec
    arrays["cst"] = shape_constants()
    at = np.clip(np.arange(P)[:, None] + T - P - np.arange(T)[None, :], -P, P) + P
    arrays["rel"] = np.ascontiguousarray(g["b_rel_bias"][0][:, at])
    return arrays


def make(nc, arrays):
    a = {n: nc.dram_tensor(f"in_{n}", v.shape, mybir.dt.from_np(v.dtype), kind="ExternalInput").ap() for n, v in arrays.items()}
    out = nc.dram_tensor("out_0", (1, T, D), F32, kind="ExternalOutput").ap()
    build(nc, a, out)


def kernel(**inputs):
    import concourse.bacc as bacc
    from concourse.bass_utils import run_bass_kernel_spmd

    arrays = lay_out(inputs)
    nc = bacc.Bacc("TRN2", target_bir_lowering=False, num_devices=1)
    make(nc, arrays)
    r = run_bass_kernel_spmd(nc, [{f"in_{n}": v for n, v in arrays.items()}], core_ids=[0])
    return r.results[0]["out_0"]
```
